# Optimizing a Trainium2 kernel written in Bass

```python
import jax, jax.numpy as jnp
from jax import lax
import numpy as np

D_MODEL = 2048
BATCH = 1
SEQ = 256
DEPTH = 2

POOL_WIDTH = D_MODEL // 2
POOL_WINDOWS = (2, 4, 8, 16)
POOL_GROUP = POOL_WIDTH // len(POOL_WINDOWS)
HEAD_DIM = 128
N_HEADS = (D_MODEL - POOL_WIDTH) // HEAD_DIM
N_KV = 2
GROUP_SIZE = N_HEADS // N_KV
ATT_WIDTH = N_HEADS * HEAD_DIM
KV_WIDTH = N_KV * HEAD_DIM
CMP_LEN = 32
CMP_STRIDE = 16
SLC_LEN = 64
SLC_TOPK = 16
WIN = 512
Q_BLOCK = 128
SLC_Q_CHUNK = 32
D_FF = -(-8 * D_MODEL // (3 * 256)) * 256
IN_COLS = POOL_WIDTH + ATT_WIDTH + 6 * KV_WIDTH + 3 * N_HEADS
NORM_EPS = 1e-6
NEG_INF = -1e30
FORCE_BONUS = 1e3

kernel_name = "hymba_pool_nsa_alibi_adaln_block"

def rmsnorm(x, g):
    x32 = x.astype(jnp.float32)
    y = x32 * lax.rsqrt(jnp.mean(x32 * x32, axis=-1, keepdims=True) + NORM_EPS)
    return (y * g.astype(jnp.float32)).astype(x.dtype)

def masked_softmax(s, mask):
    s = jnp.where(mask, s, NEG_INF)
    p = jax.nn.softmax(s, axis=-1)
    return jnp.where(mask, p, 0.0)

def alibi_slopes():
    sl = 2.0 ** (-8.0 * np.arange(1, N_HEADS + 1) / N_HEADS)
    return jnp.asarray(sl, jnp.float32).reshape(N_KV, GROUP_SIZE)

def split_points():
    sizes = [POOL_WIDTH, ATT_WIDTH] + [KV_WIDTH] * 6 + [3 * N_HEADS]
    return [int(v) for v in np.cumsum(sizes)[:-1]]

def pool_mixer(u, w_pool, pool_scale):
    B, T, _ = u.shape
    u32 = u.astype(jnp.float32)
    cs = jnp.pad(jnp.cumsum(u32, axis=1), ((0, 0), (1, 0), (0, 0)))
    t = np.arange(T)
    outs = []
    for gi, w in enumerate(POOL_WINDOWS):
        sl = slice(gi * POOL_GROUP, (gi + 1) * POOL_GROUP)
        c_g = cs[..., sl]
        lo = np.maximum(t + 1 - w, 0)
        cnt = jnp.asarray((t + 1 - lo).astype(np.float32))
        mean = (c_g[:, 1:] - c_g[:, lo]) / cnt[None, :, None]
        outs.append(mean - u32[..., sl])
    pooled = jnp.stack(outs, axis=2).astype(u.dtype)
    mixed = jnp.einsum('btgc,gcd->btgd', pooled, w_pool)
    return mixed.reshape(B, T, POOL_WIDTH) * pool_scale

def compress(k, pe, w1, w2):
    B, T, G, dh = k.shape
    n_cmp = (T - CMP_LEN) // CMP_STRIDE + 1
    idx = np.arange(n_cmp)[:, None] * CMP_STRIDE + np.arange(CMP_LEN)[None, :]
    blocks = k[:, idx] + pe[None, None, :, None, :]
    flat = blocks.transpose(0, 1, 3, 2, 4).reshape(B, n_cmp, G, CMP_LEN * dh)
    return jax.nn.silu(flat @ w1) @ w2

def nsa_mixer(q, kc, vc, ks, vs, kw, vw, gate_logits, q_gain, k_gain, pe_cmp, w_cmp1, w_cmp2):
    B, T = q.shape[:2]
    G, R, dh = N_KV, GROUP_SIZE, HEAD_DIM
    scale = dh ** -0.5
    slopes = alibi_slopes()
    qg = rmsnorm(q, q_gain).reshape(B, T, G, R, dh)
    t = np.arange(T)

    kcmp = rmsnorm(compress(kc, pe_cmp[0], w_cmp1[0], w_cmp2[0]), k_gain[0])
    vcmp = compress(vc, pe_cmp[1], w_cmp1[1], w_cmp2[1])
    n_cmp = kcmp.shape[1]
    end_pos = np.arange(n_cmp) * CMP_STRIDE + CMP_LEN - 1
    dist_c = (t[:, None] - end_pos[None, :]).astype(np.float32)
    s = jnp.einsum('btgrd,bcgd->bgrtc', qg, kcmp).astype(jnp.float32) * scale
    s = s - slopes[None, :, :, None, None] * jnp.asarray(dist_c)[None, None, None]
    p_cmp = masked_softmax(s, jnp.asarray(dist_c >= 0)[None, None, None])
    o_cmp = jnp.einsum('bgrtc,bcgd->btgrd', p_cmp.astype(vcmp.dtype), vcmp)

    n_slc = T // SLC_LEN
    n_sel = min(SLC_TOPK, n_slc)
    cst = np.arange(n_cmp) * CMP_STRIDE
    sst = np.arange(n_slc) * SLC_LEN
    overlap = ((cst[:, None] < sst[None, :] + SLC_LEN) & (cst[:, None] + CMP_LEN > sst[None, :]))
    imp = jnp.einsum('bgrtc,cs->bgts', p_cmp, jnp.asarray(overlap.astype(np.float32)))
    cur = t // SLC_LEN
    jb = np.arange(n_slc)
    valid = sst[None, :] <= t[:, None]
    forced = (jb[None, :] == 0) | (jb[None, :] == cur[:, None]) | (jb[None, :] == cur[:, None] - 1)
    score = jnp.where(jnp.asarray(valid), imp + FORCE_BONUS * jnp.asarray(forced.astype(np.float32)), NEG_INF)
    idx = lax.top_k(score, n_sel)[1]

    ks_n = rmsnorm(ks, k_gain[1])
    kblk = ks_n.reshape(B, n_slc, SLC_LEN, G, dh).transpose(0, 3, 1, 2, 4)
    vblk = vs.reshape(B, n_slc, SLC_LEN, G, dh).transpose(0, 3, 1, 2, 4)
    nq = T // SLC_Q_CHUNK
    q_ch = qg.reshape(B, nq, SLC_Q_CHUNK, G, R, dh).transpose(1, 0, 3, 2, 4, 5)
    idx_ch = idx.reshape(B, G, nq, SLC_Q_CHUNK, n_sel).transpose(2, 0, 1, 3, 4)
    t_ch = jnp.asarray(t.reshape(nq, SLC_Q_CHUNK).astype(np.int32))
    bi = jnp.arange(B)[:, None, None, None]
    gi = jnp.arange(G)[None, :, None, None]
    offs = jnp.arange(SLC_LEN, dtype=jnp.int32)

    def sel_chunk(args):
        qc, ic, tc = args
        ksel = kblk[bi, gi, ic].reshape(B, G, SLC_Q_CHUNK, n_sel * SLC_LEN, dh)
        vsel = vblk[bi, gi, ic].reshape(B, G, SLC_Q_CHUNK, n_sel * SLC_LEN, dh)
        pos = (ic[..., None] * SLC_LEN + offs).reshape(B, G, SLC_Q_CHUNK, n_sel * SLC_LEN)
        dist = tc[None, None, :, None] - pos
        sc = jnp.einsum('bgqrd,bgqkd->bgrqk', qc, ksel).astype(jnp.float32) * scale
        sc = sc - slopes[None, :, :, None, None] * dist[:, :, None].astype(jnp.float32)
        pr = masked_softmax(sc, (dist >= 0)[:, :, None])
        return jnp.einsum('bgrqk,bgqkd->bqgrd', pr.astype(vsel.dtype), vsel)

    o_slc = lax.map(sel_chunk, (q_ch, idx_ch, t_ch))
    o_slc = o_slc.transpose(1, 0, 2, 3, 4, 5).reshape(B, T, G, R, dh)

    kw_n = rmsnorm(kw, k_gain[2])
    nb = T // Q_BLOCK
    nwb = WIN // Q_BLOCK
    def band(a):
        ab = jnp.pad(a.reshape(B, nb, Q_BLOCK, G, dh), ((0, 0), (nwb, 0), (0, 0), (0, 0), (0, 0)))
        return jnp.concatenate([ab[:, i:i + nb] for i in range(nwb + 1)], axis=2)
    kband, vband = band(kw_n), band(vw)
    jq = np.arange(nb)
    kpos = (jq[:, None] - nwb) * Q_BLOCK + np.arange((nwb + 1) * Q_BLOCK)[None, :]
    tq = jq[:, None] * Q_BLOCK + np.arange(Q_BLOCK)[None, :]
    dist_w = tq[:, :, None] - kpos[:, None, :]
    mask_w = (dist_w >= 0) & (dist_w < WIN) & (kpos[:, None, :] >= 0)
    qw = qg.reshape(B, nb, Q_BLOCK, G, R, dh)
    sw = jnp.einsum('bjqgrd,bjkgd->bjgrqk', qw, kband).astype(jnp.float32) * scale
    sw = sw - slopes[None, None, :, :, None, None] * jnp.asarray(dist_w.astype(np.float32))[None, :, None, None]
    pw = masked_softmax(sw, jnp.asarray(mask_w)[None, :, None, None])
    o_win = jnp.einsum('bjgrqk,bjkgd->bjqgrd', pw.astype(vband.dtype), vband).reshape(B, T, G, R, dh)

    g = jax.nn.sigmoid(gate_logits.reshape(B, T, G, R, 3))
    o = g[..., 0:1] * o_cmp + g[..., 1:2] * o_slc + g[..., 2:3] * o_win
    return o.reshape(B, T, ATT_WIDTH)

def setup_inputs(seed: int = 0) -> dict:
    key = jax.random.key(seed)
    ks = jax.random.split(key, 17)
    f32 = jnp.float32
    nrm = lambda k, shape, s: jax.random.normal(k, shape, f32) * s
    L = DEPTH
    return {
        "x": nrm(ks[0], (BATCH, SEQ, D_MODEL), 1.0),
        "c": nrm(ks[1], (BATCH, D_MODEL), 1.0),
        "w_ada": nrm(ks[2], (L, D_MODEL, 6 * D_MODEL), 0.5 * D_MODEL ** -0.5),
        "b_ada": nrm(ks[3], (L, 6 * D_MODEL), 0.02),
        "norm_g": 1.0 + nrm(ks[4], (L, 2, D_MODEL), 0.05),
        "w_in": nrm(ks[5], (L, D_MODEL, IN_COLS), D_MODEL ** -0.5),
        "q_gain": 1.0 + nrm(ks[6], (L, HEAD_DIM), 0.05),
        "k_gain": 1.0 + nrm(ks[7], (L, 3, HEAD_DIM), 0.05),
        "pe_cmp": nrm(ks[8], (L, 2, CMP_LEN, HEAD_DIM), 0.5),
        "w_cmp1": nrm(ks[9], (L, 2, CMP_LEN * HEAD_DIM, HEAD_DIM), (CMP_LEN * HEAD_DIM) ** -0.5),
        "w_cmp2": nrm(ks[10], (L, 2, HEAD_DIM, HEAD_DIM), HEAD_DIM ** -0.5),
        "w_pool": nrm(ks[11], (L, len(POOL_WINDOWS), POOL_GROUP, POOL_GROUP), POOL_GROUP ** -0.5),
        "pool_scale": 1.0 + nrm(ks[12], (L, POOL_WIDTH), 0.05),
        "w_out": nrm(ks[13], (L, D_MODEL, D_MODEL), D_MODEL ** -0.5),
        "w_gate_up": nrm(ks[14], (L, D_MODEL, 2 * D_FF), D_MODEL ** -0.5),
        "w_down": nrm(ks[15], (L, D_FF, D_MODEL), D_FF ** -0.5),
    }

def reference(x, c, w_ada, b_ada, norm_g, w_in, q_gain, k_gain, pe_cmp, w_cmp1, w_cmp2,
              w_pool, pool_scale, w_out, w_gate_up, w_down):
    B, T, _ = x.shape
    cond = jax.nn.silu(c)
    pts = split_points()
    for l in range(DEPTH):
        mod = (cond @ w_ada[l] + b_ada[l])[:, None, :]
        sh1, sc1, g1, sh2, sc2, g2 = jnp.split(mod, 6, axis=-1)
        h = rmsnorm(x, norm_g[l, 0]) * (1.0 + sc1) + sh1
        proj = h @ w_in[l]
        u, q, kc, vc, ksl, vsl, kwn, vwn, gl = jnp.split(proj, pts, axis=-1)
        kv = lambda a: a.reshape(B, T, N_KV, HEAD_DIM)
        a_out = pool_mixer(u, w_pool[l], pool_scale[l])
        o_out = nsa_mixer(q.reshape(B, T, N_HEADS, HEAD_DIM), kv(kc), kv(vc), kv(ksl), kv(vsl),
                          kv(kwn), kv(vwn), gl, q_gain[l], k_gain[l], pe_cmp[l],
                          w_cmp1[l], w_cmp2[l])
        x = x + g1 * (jnp.concatenate([a_out, o_out], axis=-1) @ w_out[l])
        h2 = rmsnorm(x, norm_g[l, 1]) * (1.0 + sc2) + sh2
        gate, up = jnp.split(h2 @ w_gate_up[l], 2, axis=-1)
        x = x + g2 * ((jax.nn.silu(gate) * up) @ w_down[l])
    return x


_drawn_inputs = setup_inputs


def setup_inputs(seed=0):
    import zlib

    import numpy as np

    out = dict(_drawn_inputs(seed))
    spreads = {}
    factors = {'q_gain': 8.0, 'k_gain': 8.0, 'pool_scale': 4.175}
    for name, (base, spread) in spreads.items():
        noise = np.random.default_rng([zlib.crc32(name.encode()), seed]).standard_normal(out[name].shape)
        drawn = base * np.exp(spread * noise) if base else spread * noise
        out[name] = __import__('jax').numpy.asarray(drawn.astype(out[name].dtype))
    for name, factor in factors.items():
        out[name] = (out[name] * factor).astype(out[name].dtype)
    return out
```

```python
from contextlib import ExitStack

import numpy as np

import concourse.bass as bass
from concourse import mybir

ALU = mybir.AluOpType
ACT = mybir.ActivationFunctionType
F32 = mybir.dt.float32
F32R = mybir.dt.float32r
I32 = mybir.dt.int32
X = mybir.AxisListType.X

P = 128
D, T, DEPTH = 2048, 256, 2
TOKS = T // P
KT = D // P
POOL, HEADS, KV, DH = 1024, 8, 2, 128
REP = HEADS // KV
POOL_WINDOWS = (2, 4, 8, 16)
PG = POOL // len(POOL_WINDOWS)
CMP_LEN, CMP_STRIDE = 32, 16
NC = (T - CMP_LEN) // CMP_STRIDE + 1
FF = 5632
EPS = 1e-6
NEG = -1e30
COLS = 512
FCH = 256

DVE_STEPS = 143

T_KV, T_GL, T_CMP1, T_CMP2 = 0, 12, 13, 17
T_Q, T_U0, T_POOL, T_PASS2, T_MLP = 18, 26, (32, 37), 44, 52
T_U1 = (30, 31, 33, 34)
T_PASS1 = ((35, 36), (38, 39), (40, 41), (42, 43))
DIRECT = (12, 13, 14, 15, 16, 17, 32, 37)
PART_KT = 12
PARTS = 3
LAST_KT = FF // P - PARTS * PART_KT
PART_UP, LAST_UP = PART_KT // 2, LAST_KT // 2
PART_G, LAST_G = PART_KT // 4, LAST_KT // 4
PART_TILES = 4 * PART_UP + 4 * PART_G
LAST_TILES = 4 * LAST_UP + 4 * LAST_G
TILES = T_MLP + PARTS * PART_TILES + LAST_TILES
assert TILES % 4 == 0 and PART_TILES % 4 == 0 and FF % (2 * FCH) == 0


def half_of(t):
    return 2 * (t - sum(d < t for d in DIRECT))


HALVES = half_of(TILES)
PART_HALVES = 2 * PART_TILES
assert HALVES % 4 == 0

C_KV, C_GL, C_Q, C_U, C_PASS1, C_PASS2, C_MLP = 0, 3, 4, 6, 8, 12, 16
PART_CHUNKS = PART_UP + 4
CHUNKS = C_MLP + PARTS * PART_CHUNKS + LAST_UP + 4
assert CHUNKS % 2 == 0 and PART_CHUNKS % 2 == 0

PER = (25, 26, 27, 28, 29, 30, 31, 33, 34, 35, 36, 38, 39, 40, 41, 42, 43, 44)
NSTEP = 16
SIDE, MID = 0, 1
POOLED_AT = (31, 33, 36, 38)
MIX_AT = (33, 34, 38, 39)


def ordered(events):
    return {name: i for i, (_, _, name) in enumerate(sorted(events, key=lambda e: e[:2]))}


S_USE = ordered(
    [(12, 0, "hidden"), (18, 2, "cmp out"), (24, MID, "cmp scores 0"), (29, MID, "cmp scores 1"),
     (28, MID, "q 1")]
    + [(PER[n], SIDE, f"scores {n}") for n in range(NSTEP)]
    + [(PER[4 * u + 1], MID, f"cmp probs {u}") for u in range(4)]
    + [(POOLED_AT[i], MID, f"pooled {i}") for i in range(4)])
A_USE = ordered(
    [(-9 + j, 0, f"norm1 {j}") for j in range(0, 8, 2)]
    + [(5, SIDE, "kv 0"), (10, SIDE, "kv 1"), (13, SIDE, "kv 2"), (21, SIDE, "kcmp"), (24, SIDE, "q 0"),
       (28, MID, "q 1")]
    + [(PER[n + 1], SIDE, f"probs {n}") for n in range(NSTEP)]
    + [(MIX_AT[i], MID, f"mix {i}") for i in range(4)]
    + [(50 + j, 0, f"norm2 {j}") for j in range(0, 8, 2)])
B_USE = ordered(
    [(-9 + j, 0, f"norm1 {j}") for j in range(1, 8, 2)]
    + [(5, SIDE, "kv 0"), (10, SIDE, "kv 1"), (13, SIDE, "kv 2"), (24, SIDE, "q 0")]
    + [(PER[4 * u + 2], SIDE, f"heads {u}") for u in range(4)]
    + [(50 + j, 0, f"norm2 {j}") for j in range(1, 8, 2)])
A_MLP, B_MLP = len(A_USE), len(B_USE)

ST_NORM1, ST_KV, ST_KCMP, ST_Q, ST_NORM2, STAGES = 0, 8, 12, 13, 17, 25

UNITS = 12
FIRST_UNITS = 4
ADA_PERIODS = {
    0: {3: 4, 4: 3, 5: 3, 6: 3, 7: 3},
    1: {9: 4, 10: 3, 11: 3, 12: 6},
    2: {19: 4, 20: 3, 21: 3, 22: 3, 23: 3},
    3: {24: 2, 25: 2, 26: 3, 27: 3, 28: 3, 29: 3},
    4: {30: 3, 31: 3, 33: 3, 34: 3, 35: 2, 36: 2},
    5: {38: 2, 39: 2, 40: 2, 41: 2, 42: 2, 43: 2, 44: 2, 45: 2},
}
ADA_REDUCE = {0: (8, 9), 1: (18, 19), 2: (24,), 3: (30,), 4: (38,), 5: (46,)}
PART_ADA = ((0, (2, 1, 2, 1, 2, 1, 2, 1, 2, 1, 1)), (13, (2, 1, 2, 1, 2, 1, 2, 1, 2, 1, 1)))
PART_REDUCE = ((11, 12), (24, 25))

CV = {"g2": 0, "b_shift2": 16, "b_scale2": 32, "pool_scale": 48, "q_gain": 56, "k_gain": 57, "pe": 60}
CV_N = 124
NV_N = 48
K_ID, K_ONE, K_DIST, K_CMP, K_SEEN = 0, 128, 256, 512, 512 + 2 * 8 * NC
K_N = K_SEEN + 1


def constants():
    k = np.zeros((P, K_N), np.float32)
    k[:, K_ID:K_ID + P] = np.eye(P)
    k[:, K_ONE:K_ONE + P] = 1.0
    t, j = np.arange(P)[:, None], np.arange(P)[None, :]
    k[:, K_DIST:K_DIST + P] = -(P + t - j)
    k[:, K_DIST + P:K_DIST + 2 * P] = np.where(t >= j, -(t - j), -1e33)
    end = np.arange(NC) * CMP_STRIDE + CMP_LEN - 1
    cmp = k[:, K_CMP:K_SEEN].reshape(P, KV, TOKS, REP, NC)
    for g in range(KV):
        for q in range(TOKS):
            for r in range(REP):
                dist = q * P + t - end[None, :]
                cmp[:, g, q, r] = np.where(dist >= 0, -(2.0 ** -(g * REP + r + 1)) * dist, NEG)
    k[:, K_SEEN] = np.arange(P) >= end[0]
    return k


def pool_matrices():
    out = np.zeros((P, len(POOL_WINDOWS), 3 * P), np.float32)
    t = np.arange(T)
    for i, w in enumerate(POOL_WINDOWS):
        count = np.minimum(t + 1, w)
        m = np.where((t[:, None] <= t[None, :]) & (t[:, None] > t[None, :] - w), 1.0 / count[None, :], 0.0)
        m = m - np.eye(T)
        out[:, i, :T] = m[:P]
        out[:, i, T:] = m[P:, P:]
    return out


class Place:

    def __init__(self):
        self.layer = self.part = None

    def value(self, n, per_layer, per_part=0):
        if self.part is not None and per_part:
            n = self.part * per_part + n
        if self.layer is not None:
            n = self.layer * per_layer + n
        return n


class Count:

    def __init__(self, sem, per_layer, per_part=0, start=0):
        self.sem, self.per_layer, self.per_part, self.start = sem, per_layer, per_part, start

    def at(self, here, n):
        return here.value(n + self.start, self.per_layer, self.per_part)


class Bank:

    def __init__(self, tile, full, free):
        self.tile, self.full, self.free = tile, full, free


def build(nc, x_in, stream, w_ada, b_ada, vec, vec_next, c_col, const, out):
    ctx = ExitStack()
    with ctx:
        def sb(name, shape, dt=F32):
            return ctx.enter_context(nc.sbuf_tensor(name, shape, dt))

        def count(name, per_layer=0, per_part=0, start=0):
            return Count(ctx.enter_context(nc.semaphore(name)), per_layer, per_part, start)

        raw = [sb(f"raw{s}", [P, 4 * COLS]) for s in range(4)]
        whi = [sb(f"w_hi{s}", [P, 2, COLS], F32R) for s in range(4)]
        wlo = [sb(f"w_lo{s}", [P, 2, COLS], F32R) for s in range(4)]
        x = sb("x_sb", [P, TOKS, D])
        h_hi, h_lo = sb("h_hi", [P, KT, T], F32R), sb("h_lo", [P, KT, T], F32R)
        a_hi, a_lo = sb("a_hi", [P, PART_KT, T], F32R), sb("a_lo", [P, PART_KT, T], F32R)
        ada = [sb(f"ada{s}", [P, 1024]) for s in range(4)]
        acc = sb("acc", [P, 1024])
        gate = sb("gate", [P, D])
        cond = sb("cond", [P, KT])
        ccol = sb("ccol", [P, KT])
        cv, nv = sb("cv", [P, CV_N]), sb("nv", [P, NV_N])
        mod1 = sb("mod1", [P, 2, 2, KT])
        mod2 = sb("mod2", [P, 2, 2, KT])
        k_sb = sb("k_sb", [P, K_N])
        bufa = sb("bufa", [P, 2, 512])
        bufb = sb("bufb", [P, 2, 512])
        uc = sb("uc", [P, 1024])
        kT = sb("kT", [P, 2, KV, T])
        val = sb("val", [P, TOKS, 2, KV * DH])
        qT = sb("qT", [P, TOKS, HEADS, P])
        pT = sb("pT", [P, 2, 512])
        pooledT = sb("pooledT", [P, 2, T])
        pcT = sb("pcT", [NC, REP * P])
        kcT = sb("kcT", [P, KV, 16])
        vcmp = sb("vcmp", [NC, KV, DH])
        hexp, hid = sb("hexp", [P, 2 * KV * NC]), sb("hid", [P, 2 * KV * NC])
        pc = sb("pc", [P, KV, TOKS * REP, NC])
        gates = sb("gates", [P, TOKS, HEADS, 3])
        qgs = sb("qgs", [P, 1])
        ssq, rs = sb("ssq", [P, TOKS, 4]), sb("rs", [P, TOKS])
        ss = sb("ss", [P, TOKS, 4])
        root, root_err = sb("root", [P, 8]), sb("root_err", [P, 8])
        m8, f8 = sb("m8", [P, 8]), sb("f8", [P, 8])
        nmax, sums, fac = sb("nmax", [P, 2, 2]), sb("sums", [P, 2, 2]), sb("fac", [P, 2])

        ident = k_sb[:, K_ID:K_ID + P]
        ones = k_sb[:, K_ONE:K_ONE + P]

        ps = [ctx.enter_context(nc.psum_tensor(f"ps{b}", [P, 512], F32)) for b in range(8)]
        mod_ps = ps[7]

        a_uses, b_uses = A_MLP + PARTS * 3 + 2, B_MLP + PARTS * 3 + 2
        bank_s = Bank(ps[4], count("s_full", len(S_USE)), count("s_free", len(S_USE), 0, 1))
        bank_a = Bank(ps[5], count("a_full", a_uses, 3), count("a_free", a_uses, 3, 1))
        bank_b = Bank(ps[6], count("b_full", b_uses, 3), count("b_free", b_uses, 3, 1))
        raw_landed = [count(f"raw_landed{s}", 4 * TILES, 4 * PART_TILES) for s in range(4)]
        raw_free = [count(f"raw_free{s}", TILES // 4, PART_TILES // 4) for s in range(4)]
        ada_landed = [count(f"ada_landed{s}", 64 * UNITS, 128) for s in range(4)]
        first_landed = count("first_landed")
        x_landed = count("x_landed")
        cv_landed, nv_landed = count("cv_landed", 16), count("nv_landed", 16)
        gate_landed = count("gate_landed", 32)
        hi_ready = count("hi_ready", HALVES, PART_HALVES)
        lo_ready = count("lo_ready", HALVES, PART_HALVES)
        gemm_done = count("gemm_done", 2 * HALVES, 2 * PART_HALVES, 8)
        chunk_free = [count(f"chunk_free{b}", CHUNKS // 2, PART_CHUNKS // 2, 1) for b in range(4)]
        stage_ready = count("stage_ready", STAGES)
        norm_hi, h_ready = count("norm_hi", 16), count("h_ready", 16)
        x_updated = count("x_updated", 16 + 8 * PARTS + 8, 8)
        squared = count("squared", 16, 0, 8)
        silu_done = count("silu_done", 12 * PARTS + 2 * LAST_UP, 12)
        ff_hi = count("ff_hi", 6 * PARTS + LAST_UP, 6)
        cond_ready = count("cond_ready")
        acc_step = count("acc_step", 16 * UNITS, 32, 4)
        acc_summed = count("acc_summed", 2 * UNITS, 4)
        mod_free = count("mod_free", 2 * UNITS, 4, 1)
        blocks_ready = count("blocks_ready", 2)
        gl_done = count("gl_done", 1)
        hid_exp = count("hid_exp", 1)
        biased, exped, p_ready = count("biased", NSTEP), count("exped", NSTEP), count("p_ready", NSTEP)
        cmp_biased, cmp_exped, cmp_ready = count("cmp_biased", 2), count("cmp_exped", 2), count("cmp_ready", 2)
        mix_hi, heads_hi = count("mix_hi", 4), count("heads_hi", 4)
        dve_step = count("dve_step", DVE_STEPS)
        stored = count("stored")

        def chunk_bank(c, tok):
            return 2 * (c % 2) + tok

        def step_of(n):
            u = n // REP
            g, q = u // TOKS, u % TOKS
            return u, g, q, g * REP + n % REP, (q + 1) * P

        block = ctx.enter_context(nc.Block())

        @block.sync
        def _(sp):
            sp.dma_start(k_sb[:], const).then_inc(first_landed.sem, 16)
            sp.dma_start(nv[:], vec_next[0]).then_inc(first_landed.sem, 16)
            sp.dma_start(x[:], x_in.rearrange("(q p) d -> p q d", p=P)).then_inc(x_landed.sem, 16)
            flat = stream.rearrange("l t p c -> (l t) p c")
            for s in range(4):
                sp.dma_start(raw[s][:], flat[s]).then_inc(raw_landed[s].sem, 16)
            with sp.Fori(1, DEPTH * TILES // 4) as i:
                for s in range(4):
                    sp.wait_ge(raw_free[s].sem, i)
                    sp.dma_start(raw[s][:], flat[bass.ds(4 * i + s, 1)].rearrange("o p c -> (o p) c"))\
                        .then_inc(raw_landed[s].sem, 16)
            here = Place()
            sp.wait_ge(x_updated.sem, DEPTH * x_updated.per_layer)
            sp.dma_start(out.rearrange("(q p) d -> p q d", p=P), x[:]).then_inc(stored.sem, 16)
            sp.wait_ge(stored.sem, 16)

        @block.gpsimd
        def _(pool):
            rows = w_ada.rearrange("l (k p) n -> l k p n", p=P)
            with pool.Fori(0, DEPTH) as l:
                with pool.Fori(0, UNITS) as u:
                    for k in range(KT):
                        pool.wait_ge(acc_step.sem, l * (16 * UNITS) + u * 16 + (k + 1))
                        src = rows[bass.ds(l, 1), k, :, bass.ds(u * 1024, 1024)].rearrange("o p n -> (o p) n")
                        pool.dma_start(ada[k % 4][:], src).then_inc(ada_landed[k % 4].sem, 16)

        @block.tensor
        def _(pe):
            here = Place()

            def tile(t, c, rows, first, last, between=None):
                h = half_of(t)
                for a in range(2):
                    s = (h + a) % 4
                    pe.wait_ge(hi_ready.sem, hi_ready.at(here, h + a + 1))
                    pe.wait_ge(lo_ready.sem, lo_ready.at(here, h + a + 1))
                    for tok in range(TOKS):
                        b = chunk_bank(c, tok)
                        if first and a == 0:
                            pe.wait_ge(chunk_free[b].sem, chunk_free[b].at(here, c // 2))
                        for k in range(2):
                            xh, xl = rows[2 * a + k]
                            xh, xl = xh[:, tok * P:(tok + 1) * P], xl[:, tok * P:(tok + 1) * P]
                            begin = first and a == 0 and k == 0
                            end = last and a == 1 and k == 1
                            mm = pe.matmul(ps[b][:], xh, whi[s][:, k, :], start=begin, stop=False)
                            if a == 1 and tok == 0 and k == 0:
                                mm.then_inc(raw_free[t % 4].sem, 1)
                            pe.matmul(ps[b][:], xh, wlo[s][:, k, :], start=False, stop=False)
                            mm = pe.matmul(ps[b][:], xl, whi[s][:, k, :], start=False, stop=end)
                        mm.then_inc(gemm_done.sem, 1)
                    if a == 0 and between is not None:
                        between()

            def h_rows(g):
                return [(h_hi[:, 4 * g + i, :], h_lo[:, 4 * g + i, :]) for i in range(4)]

            def a_rows(g):
                return [(a_hi[:, 4 * g + i, :], a_lo[:, 4 * g + i, :]) for i in range(4)]

            def loaded(t):
                pe.wait_ge(raw_landed[t % 4].sem, raw_landed[t % 4].at(here, 16 * (t // 4 + 1)))

            def norm_turn(which, j):
                bank, uses = (bank_a, A_USE) if j % 2 == 0 else (bank_b, B_USE)
                pe.wait_ge(bank.free.sem, bank.free.at(here, uses[f"norm{which} {j}"]))
                pe.wait_ge(stage_ready.sem, stage_ready.at(here, (ST_NORM1 if which == 1 else ST_NORM2) + j + 1))
                for k in range(2):
                    for tok in range(TOKS):
                        o = (k * TOKS + tok) * P
                        mm = pe.transpose(bank.tile[:, o:o + P],
                                          bufb[:, j % 2, tok * 256 + k * P:tok * 256 + (k + 1) * P], ident)
                mm.then_inc(bank.full.sem, 1)

            def norm(which, t0, c):
                split = 8 * (which - 1)
                for j in range(3):
                    norm_turn(which, j)
                for g in range(4):
                    def between(g=g):
                        if 2 * g + 3 < 8:
                            norm_turn(which, 2 * g + 3)
                        pe.wait_ge(h_ready.sem, h_ready.at(here, split + 2 * g + 2))
                    pe.wait_ge(h_ready.sem, h_ready.at(here, split + 2 * g + 1))
                    tile(t0 + g, c, h_rows(g), g == 0, g == 3, between)
                    if 2 * g + 4 < 8:
                        norm_turn(which, 2 * g + 4)

            def stage_turn(bank, use, st, tok, n):
                pe.wait_ge(bank.free.sem, bank.free.at(here, use))
                if st is not None:
                    pe.wait_ge(stage_ready.sem, stage_ready.at(here, st + 1))
                for i in range(n):
                    mm = pe.transpose(bank.tile[:, i * P:(i + 1) * P], bufb[:, tok, i * P:(i + 1) * P], ident)
                mm.then_inc(bank.full.sem, 1)

            def gate_logits():
                loaded(T_GL)
                for tok in range(TOKS):
                    b = chunk_bank(C_GL, tok)
                    pe.wait_ge(chunk_free[b].sem, chunk_free[b].at(here, C_GL // 2))
                    for k in range(KT):
                        for i, part in enumerate((h_hi, h_lo)):
                            mm = pe.matmul(ps[b][:, 0:24], part[:, k, tok * P:(tok + 1) * P].bitcast(F32),
                                           raw[T_GL % 4][:, 24 * k:24 * (k + 1)],
                                           start=(k == 0 and i == 0), stop=(k == KT - 1 and i == 1))
                mm.then_inc(gl_done.sem, 1)

            def hidden(i):
                if i == 0:
                    pe.wait_ge(bank_s.free.sem, bank_s.free.at(here, S_USE["hidden"]))
                pe.wait_ge(blocks_ready.sem, blocks_ready.at(here, i + 1))
                blk = (bufa, pT)[i][:].rearrange("p a b -> p (a b)")[:, 0:KV * NC * CMP_LEN]\
                    .rearrange("p (n s) -> p n s", s=CMP_LEN)
                for pos in range(CMP_LEN):
                    t = T_CMP1 + 2 * i + pos // 16
                    if pos % 16 == 0:
                        loaded(t)
                    mm = pe.matmul(bank_s.tile[:, i * KV * NC:(i + 1) * KV * NC],
                                   raw[t % 4][:, (pos % 16) * P:(pos % 16 + 1) * P], blk[:, :, pos],
                                   start=(pos == 0), stop=(pos == CMP_LEN - 1))
                    if pos == 15 or (pos == 31 and i == 0):
                        mm.then_inc(raw_free[t % 4].sem, 1)
                if i == 1:
                    mm.then_inc(bank_s.full.sem, 1)

            def cmp_out():
                pe.wait_ge(bank_s.free.sem, bank_s.free.at(here, S_USE["cmp out"]))
                pe.wait_ge(bank_s.free.sem, bank_s.free.at(here, S_USE["hidden"] + 1))
                loaded(T_CMP2)
                for i in range(2):
                    for g in range(KV):
                        o = (i * KV + g) * DH
                        mm = pe.matmul(bank_s.tile[0:NC, o:o + DH],
                                       hid[:, (i * KV + g) * NC:(i * KV + g + 1) * NC],
                                       raw[T_CMP2 % 4][:, i * DH:(i + 1) * DH], start=True, stop=True)
                mm.then_inc(bank_s.full.sem, 1)

            def kcmp_turn():
                pe.wait_ge(bank_a.free.sem, bank_a.free.at(here, A_USE["kcmp"]))
                pe.wait_ge(stage_ready.sem, stage_ready.at(here, ST_KCMP + 1))
                for g in range(KV):
                    mm = pe.transpose(bank_a.tile[:, g * P:(g + 1) * P], bufa[:, 0, g * DH:(g + 1) * DH], ident)
                mm.then_inc(bank_a.full.sem, 1)

            def cmp_scores(g):
                pe.wait_ge(bank_s.free.sem, bank_s.free.at(here, S_USE[f"cmp scores {g}"]))
                pe.wait_ge(bank_a.free.sem, bank_a.free.at(here, A_USE["kcmp"] + 1))
                pe.wait_ge(bank_a.free.sem, bank_a.free.at(here, A_USE[f"q {g}"] + 1))
                if g == 0:
                    pe.wait_ge(bank_b.free.sem, bank_b.free.at(here, B_USE["q 0"] + 1))
                else:
                    pe.wait_ge(bank_s.free.sem, bank_s.free.at(here, S_USE["q 1"] + 1))
                for q in range(TOKS):
                    for r in range(REP):
                        o = (q * REP + r) * NC
                        mm = pe.matmul(bank_s.tile[:, o:o + NC], qT[:, q, g * REP + r, :], kcT[:, g, 0:NC],
                                       start=True, stop=True)
                mm.then_inc(bank_s.full.sem, 1)

            def scores(n):
                u, g, q, h, nk = step_of(n)
                pe.wait_ge(bank_s.free.sem, bank_s.free.at(here, S_USE[f"scores {n}"]))
                if n == 0:
                    pe.wait_ge(bank_a.free.sem, bank_a.free.at(here, A_USE["kv 2"] + 1))
                    pe.wait_ge(bank_b.free.sem, bank_b.free.at(here, B_USE["kv 2"] + 1))
                pe.matmul(bank_s.tile[:, 0:2 * nk], qT[:, q, h, :], kT[:, :, g, 0:nk], start=True,
                          stop=True).then_inc(bank_s.full.sem, 1)

            def probs_turn(n):
                u, g, q, h, nk = step_of(n)
                pe.wait_ge(bank_a.free.sem, bank_a.free.at(here, A_USE[f"probs {n}"]))
                pe.wait_ge(p_ready.sem, p_ready.at(here, n + 1))
                for i in range(2 * nk // P):
                    mm = pe.transpose(bank_a.tile[:, i * P:(i + 1) * P], bufa[:, n % 2, i * P:(i + 1) * P],
                                      ident)
                mm.then_inc(bank_a.full.sem, 1)

            def cmp_probs_turn(u):
                g, q = u // TOKS, u % TOKS
                pe.wait_ge(bank_s.free.sem, bank_s.free.at(here, S_USE[f"cmp probs {u}"]))
                pe.wait_ge(cmp_ready.sem, cmp_ready.at(here, g + 1))
                for r in range(REP):
                    mm = pe.transpose(bank_s.tile[0:NC, r * P:(r + 1) * P], pc[:, g, q * REP + r, :], ident)
                mm.then_inc(bank_s.full.sem, 1)

            def head_out(n):
                u, g, q, h, nk = step_of(n)
                r = n % REP
                if r == 0:
                    pe.wait_ge(bank_b.free.sem, bank_b.free.at(here, B_USE[f"heads {u}"]))
                    pe.wait_ge(bank_s.free.sem, bank_s.free.at(here, S_USE[f"cmp probs {u}"] + 1))
                pe.wait_ge(bank_a.free.sem, bank_a.free.at(here, A_USE[f"probs {n}"] + 1))
                o = bank_b.tile[:, r * P:(r + 1) * P]
                nb = nk // P
                for b in range(2):
                    for kb in range(nb):
                        i = b * nb + kb
                        pe.matmul(o, val[:, kb, b, g * DH:(g + 1) * DH], pT[:, n % 2, i * P:(i + 1) * P],
                                  start=(i == 0), stop=False)
                mm = pe.matmul(o, vcmp[:, g, :], pcT[:, r * P:(r + 1) * P], start=False, stop=True)
                if r == REP - 1:
                    mm.then_inc(bank_b.full.sem, 1)

            def attention_side(t):
                if t not in PER:
                    return
                m = PER.index(t)
                if 1 <= m <= NSTEP:
                    probs_turn(m - 1)
                if 2 <= m:
                    head_out(m - 2)
                if m < NSTEP:
                    scores(m)

            def pooled(i):
                pe.wait_ge(bank_s.free.sem, bank_s.free.at(here, S_USE[f"pooled {i}"]))
                t = T_POOL[i // 2]
                loaded(t)
                for tok in range(TOKS):
                    b = chunk_bank(C_U + i // 2, tok)
                    pe.wait_ge(chunk_free[b].sem, chunk_free[b].at(here, (C_U + i // 2) // 2 + 1))
                m = raw[t % 4][:, (i % 2) * 384:(i % 2 + 1) * 384]
                for k in range(2):
                    for tok in range(TOKS):
                        lhs = uc[:, tok * 512 + (i % 2) * PG + k * P:tok * 512 + (i % 2) * PG + (k + 1) * P]
                        o = k * T + tok * P
                        mm = pe.matmul(bank_s.tile[:, o:(k + 1) * T], lhs,
                                       m[:, 0:T] if tok == 0 else m[:, T:T + P],
                                       start=(tok == 0), stop=(tok == 1))
                mm.then_inc(bank_s.full.sem, 1)

            def mix(i):
                pe.wait_ge(bank_a.free.sem, bank_a.free.at(here, A_USE[f"mix {i}"]))
                pe.wait_ge(bank_s.free.sem, bank_s.free.at(here, S_USE[f"pooled {i}"] + 1))
                w = raw[T_POOL[i // 2] % 4][:, 768:1792].rearrange("p (g k c) -> p g k c", g=2, k=2)
                for d in range(2):
                    for k in range(2):
                        mm = pe.matmul(bank_a.tile[:, d * T:(d + 1) * T], w[:, i % 2, k, d * P:(d + 1) * P],
                                       pooledT[:, k, :], start=(k == 0), stop=(k == 1))
                mm.then_inc(bank_a.full.sem, 1)

            def unit_summed(q):
                pe.wait_ge(acc_step.sem, acc_step.at(here, 16 * (q + 1)))

            def columns(q):
                unit_summed(q)
                pe.wait_ge(mod_free.sem, mod_free.at(here, 2 * q))
                for k in range(8):
                    mm = pe.matmul(mod_ps[:, k:k + 1], acc[:, k * P:(k + 1) * P], ones[:, 0:1],
                                   start=True, stop=True)
                mm.then_inc(acc_summed.sem, 2)

            def spread(q, half):
                if half == 0:
                    unit_summed(q)
                pe.wait_ge(mod_free.sem, mod_free.at(here, 2 * q + half))
                pe.matmul(mod_ps[:], ones, acc[:, half * 512:(half + 1) * 512], start=True,
                          stop=True).then_inc(acc_summed.sem, 1)

            def reduce_at(t):
                for q, at in ADA_REDUCE.items():
                    if t in at:
                        if q < 2:
                            spread(FIRST_UNITS + q, at.index(t))
                        else:
                            columns(FIRST_UNITS + q)

            def middle(t):
                if t == 24:
                    cmp_scores(0)
                if t == 28:
                    stage_turn(bank_a, A_USE["q 1"], ST_Q + 2, 0, 4)
                    stage_turn(bank_s, S_USE["q 1"], ST_Q + 3, 1, 4)
                if t == 29:
                    cmp_scores(1)
                for u in range(4):
                    if t == PER[4 * u + 1]:
                        cmp_probs_turn(u)
                for i in range(4):
                    if t == MIX_AT[i]:
                        mix(i)
                for i in range(4):
                    if t == POOLED_AT[i]:
                        pooled(i)
                reduce_at(t)

            def mlp_part(o, ups, groups, sums):
                t0, c0 = T_MLP + o * PART_TILES, C_MLP + o * PART_CHUNKS

                def use(k):
                    return (A_MLP, B_MLP)[k % 2] + 3 * o + k // 2

                def bank_of(k):
                    return bank_a if k % 2 == 0 else bank_b

                def turn(k):
                    pe.wait_ge(bank_of(k).free.sem, bank_of(k).free.at(here, use(k)))
                    for tok in range(TOKS):
                        b = chunk_bank(c0 + k, tok)
                        pe.wait_ge(chunk_free[b].sem, chunk_free[b].at(here, (c0 + k) // 2 + 1))
                    for i in range(2):
                        for tok in range(TOKS):
                            at = (i * TOKS + tok) * P
                            src = tok * 256 + i * P
                            mm = pe.transpose(bank_of(k).tile[:, at:at + P], bufb[:, k % 2, src:src + P], ident)
                    mm.then_inc(bank_of(k).full.sem, 1)

                def middle(m):
                    if m % 4 == 0 and 1 <= m // 4 <= ups:
                        turn(m // 4 - 1)
                    sums(m)

                if o == 0:
                    norm(2, t0, c0)
                for m in range(4 if o == 0 else 0, 4 * ups):
                    tile(t0 + m, c0 + m // 4, h_rows(m % 4), m % 4 == 0, m % 4 == 3, lambda m=m: middle(m))
                for m in range(4 * ups, 4 * (ups + groups)):
                    n, g = divmod(m - 4 * ups, groups)
                    if n == 0:
                        for k in (2 * g, 2 * g + 1):
                            pe.wait_ge(bank_of(k).free.sem, bank_of(k).free.at(here, use(k) + 1))
                    tile(t0 + m, c0 + ups + n, a_rows(g), g == 0, g == groups - 1, lambda m=m: middle(m))

            def gate2_sums(m):
                for i, at in enumerate(PART_REDUCE):
                    if m in at:
                        spread(FIRST_UNITS + 6 + i, at.index(m))

            def next_sums(m):
                for i, at in enumerate(PART_REDUCE):
                    if m == at[0]:
                        with pe.If(here.layer < DEPTH - 1):
                            columns(FIRST_UNITS + 8 + i)

            pe.sem_inc(gemm_done.sem, 8)
            for b in range(4):
                pe.sem_inc(chunk_free[b].sem, 1)
            for bank in (bank_s, bank_a, bank_b):
                pe.sem_inc(bank.free.sem, 1)
            pe.sem_inc(mod_free.sem, 1)
            pe.wait_ge(first_landed.sem, 32)
            for q in range(FIRST_UNITS):
                columns(q)

            with pe.Fori(0, DEPTH) as layer:
                here.layer = layer
                norm(1, T_KV, C_KV)
                for t in range(4, 12):
                    if t == 5:
                        for tok, (bank, uses) in enumerate(((bank_a, A_USE), (bank_b, B_USE))):
                            b = chunk_bank(C_KV, tok)
                            pe.wait_ge(chunk_free[b].sem, chunk_free[b].at(here, C_KV // 2 + 1))
                            stage_turn(bank, uses["kv 0"], None, tok, 4)
                    if t == 10:
                        stage_turn(bank_a, A_USE["kv 1"], ST_KV, 0, 2)
                        stage_turn(bank_b, B_USE["kv 1"], ST_KV + 1, 1, 2)
                    tile(t, C_KV + t // 4, h_rows(t % 4), t % 4 == 0, t % 4 == 3, lambda t=t: middle(t))
                gate_logits()
                hidden(0)
                stage_turn(bank_a, A_USE["kv 2"], ST_KV + 2, 0, 2)
                stage_turn(bank_b, B_USE["kv 2"], ST_KV + 3, 1, 2)
                hidden(1)
                for t in range(18, 26):
                    if t == 19:
                        cmp_out()
                    if t == 21:
                        kcmp_turn()
                    if t == 24:
                        stage_turn(bank_a, A_USE["q 0"], ST_Q, 0, 4)
                        stage_turn(bank_b, B_USE["q 0"], ST_Q + 1, 1, 4)
                    attention_side(t)
                    g = (t - 18) % 4
                    tile(t, C_Q + (t - 18) // 4, h_rows(g), g == 0, g == 3, lambda t=t: middle(t))
                for i, t in enumerate((26, 27, 28, 29) + T_U1):
                    attention_side(t)
                    g = i % 4
                    tile(t, C_U + i // 4, h_rows(g), g == 0, g == 3, lambda t=t: middle(t))
                for n, tiles in enumerate(T_PASS1):
                    for i, t in enumerate(tiles):
                        attention_side(t)
                        if n == 0 and i == 0:
                            for j in (0, 1):
                                pe.wait_ge(bank_a.free.sem, bank_a.free.at(here, A_USE[f"mix {j}"] + 1))
                        if n == 0 and i == 1:
                            for u in (0, 1):
                                pe.wait_ge(bank_b.free.sem, bank_b.free.at(here, B_USE[f"heads {u}"] + 1))
                        tile(t, C_PASS1 + n, a_rows(2 * i), i == 0, i == 1, lambda t=t: middle(t))
                for n in range(4):
                    for i in range(2):
                        t = T_PASS2 + 2 * n + i
                        attention_side(t)
                        if n == 0 and i == 0:
                            for j in (2, 3):
                                pe.wait_ge(bank_a.free.sem, bank_a.free.at(here, A_USE[f"mix {j}"] + 1))
                        if n == 0 and i == 1:
                            for u in (2, 3):
                                pe.wait_ge(bank_b.free.sem, bank_b.free.at(here, B_USE[f"heads {u}"] + 1))
                        rows = a_rows(1) if i == 0 else h_rows(0)
                        tile(t, C_PASS2 + n, rows, i == 0, i == 1, lambda t=t: middle(t))
                mlp_part(0, PART_UP, PART_G, gate2_sums)
                with pe.Fori(0, PARTS - 1) as part:
                    here.part = part
                    mlp_part(1, PART_UP, PART_G, next_sums)
                here.part = None
                mlp_part(PARTS, LAST_UP, LAST_G, lambda m: None)

        @block.scalar
        def _(act):
            here = Place()

            def split_hi(t, a):
                h = half_of(t) + a
                if a == 0:
                    act.wait_ge(raw_landed[t % 4].sem, raw_landed[t % 4].at(here, 16 * (t // 4 + 1)))
                act.wait_ge(gemm_done.sem, gemm_done.at(here, 2 * h - 6))
                act.activation(whi[h % 4][:].rearrange("p k c -> p (k c)"),
                               raw[t % 4][:, a * 1024:(a + 1) * 1024], ACT.Copy).then_inc(hi_ready.sem, 1)

            def chunk_done(t, tok):
                act.wait_ge(gemm_done.sem, gemm_done.at(here, 2 * half_of(t) + 2 + tok + 1))

            def copy_chunk(t, c, dst):
                for tok in range(TOKS):
                    chunk_done(t, tok)
                    act.activation(dst(tok), ps[chunk_bank(c, tok)][:], ACT.Copy)\
                        .then_inc(chunk_free[chunk_bank(c, tok)].sem, 1)

            def copy_keys(t, c, branch):
                for tok in range(TOKS):
                    chunk_done(t, tok)
                    bank = ps[chunk_bank(c, tok)]
                    act.activation(val[:, tok, branch, :], bank[:, 256:512], ACT.Copy)
                    act.activation(bufb[:, tok, 0:256], bank[:, 0:256], ACT.Copy)\
                        .then_inc(chunk_free[chunk_bank(c, tok)].sem, 1)

            def take(bank, use, dst, src, scale=1.0):
                act.wait_ge(bank.full.sem, bank.full.at(here, use + 1))
                act.activation(dst, src, ACT.Copy, scale=scale).then_inc(bank.free.sem, 1)

            def norm(which, t0):
                split_hi(t0, 0)
                split_hi(t0, 1)
                bank_uses = ((bank_a, A_USE), (bank_b, B_USE))
                for j in range(8):
                    bank, uses = bank_uses[j % 2]
                    act.wait_ge(bank.free.sem, bank.free.at(here, uses[f"norm{which} {j}"] + 1))
                    act.activation(h_hi[:, 2 * j:2 * j + 2, :].rearrange("p k t -> p (k t)"), bufa[:, j % 2, :],
                                   ACT.Copy).then_inc(norm_hi.sem, 1)
                    if j + 2 < 8:
                        split_hi(t0 + (j + 2) // 2, j % 2)

            def square(i, n, tok, updated):
                if updated is not None:
                    act.wait_ge(x_updated.sem, x_updated.at(here, updated))
                act.wait_ge(squared.sem, squared.at(here, i - 1))
                act.activation(h_hi[:, 8 + 2 * tok:10 + 2 * tok, :].rearrange("p k t -> p (k t)"),
                               x[:, tok, n * 512:(n + 1) * 512], ACT.Square,
                               accum_out=ssq[:, tok, n:n + 1]).then_inc(squared.sem, 1)

            def exp(n):
                u, g, q, h, nk = step_of(n)
                act.wait_ge(biased.sem, biased.at(here, n + 1))
                for b in range(2):
                    row = bufa[:, n % 2, b * nk:(b + 1) * nk]
                    last = act.activation(row, row, ACT.Exp, bias=nmax[:, n % 2, b:b + 1],
                                          accum_out=sums[:, n % 2, b:b + 1])
                last.then_inc(exped.sem, 1)

            def cmp_exp(g):
                act.wait_ge(cmp_biased.sem, cmp_biased.at(here, g + 1))
                row = pc[:, g].rearrange("p n c -> p (n c)")
                act.activation(row, row, ACT.Exp).then_inc(cmp_exped.sem, 1)

            def heads_to_rows(u):
                g, q = u // TOKS, u % TOKS
                act.wait_ge(bank_b.full.sem, bank_b.full.at(here, B_USE[f"heads {u}"] + 1))
                dst = a_hi[:, 8:12, q * P:(q + 1) * P] if g == 0 else h_hi[:, 0:4, q * P:(q + 1) * P]
                act.activation(dst, bank_b.tile[:].rearrange("p (r t) -> p r t", r=REP), ACT.Copy)\
                    .then_inc(heads_hi.sem, 1)

            def mixed(i):
                act.wait_ge(bank_a.full.sem, bank_a.full.at(here, A_USE[f"mix {i}"] + 1))
                if i % 2 == 1:
                    act.sem_inc(raw_free[T_POOL[i // 2] % 4].sem, 1)
                for d in range(2):
                    k = 2 * i + d
                    last = act.activation(a_hi[:, k, :], bank_a.tile[:, d * T:(d + 1) * T], ACT.Copy,
                                          scale=cv[:, CV["pool_scale"] + k:CV["pool_scale"] + k + 1])
                last.then_inc(mix_hi.sem, 1)

            def period(t, nxt):
                m = PER.index(t) if t in PER else -1
                if t == 4:
                    copy_chunk(3, C_KV, lambda tok: bufb[:, tok, :])
                if t == 5:
                    for tok, (bank, uses) in enumerate(((bank_a, A_USE), (bank_b, B_USE))):
                        take(bank, uses["kv 0"],
                             uc[:].rearrange("p (n t) -> p n t", n=4)[:, :, tok * P:(tok + 1) * P],
                             bank.tile[:].rearrange("p (n t) -> p n t", n=4))
                if t == 8:
                    copy_keys(7, C_KV + 1, 0)
                if t == 10:
                    act.wait_ge(cv_landed.sem, cv_landed.at(here, 16))
                    take_keys(0)
                if t == 21:
                    take(bank_a, A_USE["kcmp"], kcT[:, :, 0:NC],
                         bank_a.tile[:, 0:KV * P].rearrange("p (g c) -> p g c", g=KV)[:, :, 0:NC],
                         cv[:, CV["k_gain"]:CV["k_gain"] + 1])
                if t == 22:
                    copy_chunk(21, C_Q, lambda tok: bufb[:, tok, :])
                if t == 24:
                    take_queries(0, ((bank_a, A_USE), (bank_b, B_USE)))
                if t == 26:
                    copy_chunk(25, C_Q + 1, lambda tok: bufb[:, tok, :])
                if 1 <= m <= NSTEP:
                    n = m - 1
                    nk = step_of(n)[4]
                    take(bank_a, A_USE[f"probs {n}"], pT[:, n % 2, 0:2 * nk], bank_a.tile[:, 0:2 * nk])
                if t == 30:
                    copy_chunk(29, C_U, lambda tok: uc[:, tok * 512:(tok + 1) * 512])
                if t == 35:
                    copy_chunk(34, C_U + 1, lambda tok: uc[:, tok * 512:(tok + 1) * 512])
                for u in range(4):
                    if t == PER[4 * u + 5]:
                        heads_to_rows(u)
                if nxt is not None:
                    split_hi(nxt, 0)
                if 0 <= m < NSTEP:
                    exp(m)
                if nxt is not None:
                    split_hi(nxt, 1)
                if t == 24:
                    cmp_exp(0)
                if t == 28:
                    take_queries(1, ((bank_a, A_USE), (bank_s, S_USE)))
                if t == 29:
                    cmp_exp(1)
                for u in range(4):
                    if t == PER[4 * u + 1]:
                        take(bank_s, S_USE[f"cmp probs {u}"], pcT[:], bank_s.tile[0:NC, :])
                for i in range(4):
                    if t == MIX_AT[i]:
                        mixed(i)
                for i in range(4):
                    if t == POOLED_AT[i]:
                        take(bank_s, S_USE[f"pooled {i}"], pooledT[:].rearrange("p k t -> p (k t)"),
                             bank_s.tile[:])
                if t in (46, 48, 50):
                    n = (t - 46) // 2
                    for tok in range(TOKS):
                        square(2 * n + tok, n, tok, 8 + 2 * n + tok + 1)

            def take_keys(branch):
                for tok, (bank, uses) in enumerate(((bank_a, A_USE), (bank_b, B_USE))):
                    take(bank, uses[f"kv {branch + 1}"], kT[:, branch, :, tok * P:(tok + 1) * P],
                         bank.tile[:, 0:256].rearrange("p (g t) -> p g t", g=KV),
                         cv[:, CV["k_gain"] + 1 + branch:CV["k_gain"] + 2 + branch])

            def take_queries(g, banks):
                for tok, (bank, uses) in enumerate(banks):
                    take(bank, uses[f"q {g}"], qT[:, tok, REP * g:REP * (g + 1), :],
                         bank.tile[:].rearrange("p (r t) -> p r t", r=REP), qgs[:, 0:1])

            def direct():
                copy_keys(11, C_KV + 2, 1)
                act.wait_ge(gl_done.sem, gl_done.at(here, 1))
                act.sem_inc(raw_free[T_GL % 4].sem, 1)
                for tok in range(TOKS):
                    b = chunk_bank(C_GL, tok)
                    act.activation(gates[:, tok].rearrange("p h b -> p (h b)"), ps[b][:, 0:24], ACT.Exp,
                                   scale=-1.0).then_inc(chunk_free[b].sem, 1)
                take_keys(1)
                act.wait_ge(bank_s.full.sem, bank_s.full.at(here, S_USE["hidden"] + 1))
                act.sem_inc(raw_free[(T_CMP1 + 3) % 4].sem, 1)
                act.activation(hexp[:], bank_s.tile[:, 0:2 * KV * NC], ACT.Exp, scale=-1.0)\
                    .then_inc(hid_exp.sem, 1)

            def mlp_part(o, ups, groups, last):
                t0, c0 = T_MLP + o * PART_TILES, C_MLP + o * PART_CHUNKS
                tiles = 4 * (ups + groups)

                def silu(k):
                    if k == 0 and o > 0:
                        act.wait_ge(x_updated.sem, x_updated.at(here, 16 + 8 * o))
                    for tok in range(TOKS):
                        if k >= 2:
                            b = chunk_bank(c0 + k, tok)
                            act.wait_ge(chunk_free[b].sem, chunk_free[b].at(here, (c0 + k - 2) // 2 + 1))
                        chunk_done(t0 + 4 * k + 3, tok)
                        act.activation(bufa[:, k % 2, tok * 256:(tok + 1) * 256],
                                       ps[chunk_bank(c0 + k, tok)][:, 0:256], ACT.Silu)\
                            .then_inc(silu_done.sem, 1)

                def rows(k):
                    bank, base = (bank_a, A_MLP) if k % 2 == 0 else (bank_b, B_MLP)
                    act.wait_ge(bank.full.sem, bank.full.at(here, base + 3 * o + k // 2 + 1))
                    act.activation(a_hi[:, 2 * k:2 * k + 2, :].rearrange("p k t -> p (k t)"), bank.tile[:],
                                   ACT.Copy).then_inc(ff_hi.sem, 1)

                for m in range(3 if o == 0 else 0, tiles):
                    k = m // 4 - 1
                    if m % 4 == 0 and 0 <= k < ups:
                        silu(k)
                    n = (m - 4 * ups) // groups - 1
                    if last and m >= 4 * ups and (m - 4 * ups) % groups == 0 and 0 <= n:
                        for tok in range(TOKS):
                            square(8 + 2 * n + tok, n, tok, 16 + 8 * o + 2 * n + tok + 1)
                    if not (last and m == tiles - 1):
                        split_hi(t0 + m + 1, 0)
                        split_hi(t0 + m + 1, 1)
                    if m % 4 == 0 and 0 <= k < ups:
                        rows(k)
                if last:
                    for tok in range(TOKS):
                        square(14 + tok, 3, tok, 16 + 8 * o + 6 + tok + 1)

            act.dma_start(ccol[:], c_col).then_inc(cond_ready.sem, 16)
            act.wait_ge(cond_ready.sem, 16)
            act.activation(cond[:], ccol[:], ACT.Silu).then_inc(cond_ready.sem, 1)
            act.wait_ge(x_landed.sem, 16)
            for n in range(4):
                for tok in range(TOKS):
                    i = 2 * n + tok
                    if i >= 2:
                        act.wait_ge(squared.sem, i - 1)
                    act.activation(h_hi[:, 8 + 2 * tok:10 + 2 * tok, :].rearrange("p k t -> p (k t)"),
                                   x[:, tok, n * 512:(n + 1) * 512], ACT.Square,
                                   accum_out=ssq[:, tok, n:n + 1]).then_inc(squared.sem, 1)

            with act.Fori(0, DEPTH) as layer:
                here.layer = layer
                norm(1, 0)
                act.dma_start(cv[:], vec[bass.ds(layer, 1)].rearrange("o p c -> (o p) c"))\
                    .then_inc(cv_landed.sem, 16)
                act.dma_start(nv[:], vec_next[bass.ds(layer + 1, 1)].rearrange("o p c -> (o p) c"))\
                    .then_inc(nv_landed.sem, 16)
                act.dma_start(gate[:], b_ada[bass.ds(layer, 1), 2 * D:3 * D].partition_broadcast(P))\
                    .then_inc(gate_landed.sem, 16)
                for t in range(3, 12):
                    period(t, t + 1 if t < 11 else None)
                direct()
                split_hi(T_Q, 0)
                split_hi(T_Q, 1)
                split_tiles = [t for t in range(T_Q, T_MLP) if t not in DIRECT]
                for i, t in enumerate(split_tiles):
                    period(t, split_tiles[i + 1] if i + 1 < len(split_tiles) else None)
                for tok in range(TOKS):
                    square(6 + tok, 3, tok, 8 + 6 + tok + 1)
                norm(2, T_MLP)
                act.dma_start(gate[:], b_ada[bass.ds(layer, 1), 5 * D:6 * D].partition_broadcast(P))\
                    .then_inc(gate_landed.sem, 16)
                mlp_part(0, PART_UP, PART_G, False)
                with act.Fori(0, PARTS - 1) as part:
                    here.part = part
                    mlp_part(1, PART_UP, PART_G, False)
                here.part = None
                mlp_part(PARTS, LAST_UP, LAST_G, True)

        @block.vector
        def _(dve):
            here = Place()
            steps = [0]

            def step():
                steps[0] += 1
                return dve_step.at(here, steps[0])

            def split_lo(t, a):
                h = half_of(t) + a
                dve.wait_ge(hi_ready.sem, hi_ready.at(here, h + 1))
                dve.tensor_tensor(wlo[h % 4][:].rearrange("p k c -> p (k c)"),
                                  raw[t % 4][:, a * 1024:(a + 1) * 1024],
                                  whi[h % 4][:].rearrange("p k c -> p (k c)").bitcast(F32), ALU.subtract)\
                    .then_inc(lo_ready.sem, 1)

            def ada_sum(q, k):
                dve.wait_ge(ada_landed[k % 4].sem, ada_landed[k % 4].at(here, 64 * q + 16 * (k // 4 + 1)))
                if k == 0:
                    if here.layer is not None or q > 0:
                        dve.wait_ge(acc_summed.sem, acc_summed.at(here, 2 * q))
                    dve.tensor_scalar(acc[:], ada[0][:], cond[:, 0:1], None, ALU.mult).then_inc(acc_step.sem, 1)
                    return
                dve.wait_ge(acc_step.sem, acc_step.at(here, 16 * q + k))
                dve.scalar_tensor_tensor(acc[:], ada[k % 4][:], cond[:, k:k + 1], acc[:], ALU.mult, ALU.add)\
                    .then_inc(acc_step.sem, 1)

            def take_columns(q, table, bias, gain):
                dve.wait_ge(acc_summed.sem, acc_summed.at(here, 2 * q + 2))
                half = (q % 2) * 8
                plain, scaled = table[:, 0, half:half + 8], table[:, 1, half:half + 8]
                dve.tensor_tensor(plain, mod_ps[:, 0:8], bias[:, half:half + 8], ALU.add)\
                    .then_inc(mod_free.sem, 2)
                dve.wait_ge(mod_free.sem, mod_free.at(here, 2 * q + 2))
                dve.scalar_tensor_tensor(scaled, plain, 1.0, gain[:, half:half + 8], ALU.add, ALU.mult)

            def take_spread(q, step):
                if q % 2 == 0 and step == 0:
                    dve.wait_ge(gate_landed.sem, gate_landed.at(here, 16 if q < FIRST_UNITS + 6 else 32))
                dve.wait_ge(acc_summed.sem, acc_summed.at(here, 2 * q + step + 1))
                g = gate[:, (q % 2) * 1024 + step * 512:(q % 2) * 1024 + (step + 1) * 512]
                dve.tensor_tensor(g, mod_ps[:], g, ALU.add).then_inc(mod_free.sem, 1)

            def rstd(v, width):
                y, e = root[0:v.shape[0]], root_err[0:v.shape[0]]
                if len(v.shape) == 3:
                    y, e = (r.rearrange("p (q n) -> p q n", q=TOKS)[:, :, 0:v.shape[2]] for r in (y, e))
                else:
                    y, e = y[:, 0:v.shape[1]], e[:, 0:v.shape[1]]
                dve.tensor_scalar(v, v, 1.0 / width, EPS, ALU.mult, ALU.add).then_inc(dve_step.sem, 1)
                dve.wait_ge(dve_step.sem, step())
                dve.tensor_scalar(y.bitcast(I32), v.bitcast(I32), -0.5, float(0x5f3759df), ALU.mult, ALU.add)\
                    .then_inc(dve_step.sem, 1)
                dve.wait_ge(dve_step.sem, step())
                for i in range(3):
                    dve.tensor_tensor(e, y, y, ALU.mult).then_inc(dve_step.sem, 1)
                    dve.wait_ge(dve_step.sem, step())
                    dve.scalar_tensor_tensor(e, e, -0.5, v, ALU.mult, ALU.mult).then_inc(dve_step.sem, 1)
                    dve.wait_ge(dve_step.sem, step())
                    dve.scalar_tensor_tensor(v if i == 2 else y, e, 1.5, y, ALU.add, ALU.mult)\
                        .then_inc(dve_step.sem, 1)
                    dve.wait_ge(dve_step.sem, step())

            def norm(which, t0, mod):
                dve.wait_ge(squared.sem, squared.at(here, 0 if which == 1 else 8))
                dve.tensor_reduce(rs[:], ssq[:], X, ALU.add).then_inc(dve_step.sem, 1)
                dve.wait_ge(dve_step.sem, step())
                rstd(rs[:], D)
                uses = (A_USE, B_USE)
                banks = (bank_a, bank_b)

                def stage(j):
                    if j >= 2:
                        use = uses[j % 2][f"norm{which} {j - 2}"]
                        dve.wait_ge(banks[j % 2].full.sem, banks[j % 2].full.at(here, use + 1))
                    for tok in range(TOKS):
                        last = dve.tensor_scalar(bufb[:, j % 2, tok * 256:(tok + 1) * 256],
                                                 x[:, tok, j * 256:(j + 1) * 256], rs[:, tok:tok + 1], None,
                                                 ALU.mult)
                    last.then_inc(stage_ready.sem, 1)

                stage(0)
                stage(1)
                split_lo(t0, 0)
                shift, scale = mod
                for j in range(8):
                    bank, use = banks[j % 2], uses[j % 2][f"norm{which} {j}"]
                    dve.wait_ge(bank.full.sem, bank.full.at(here, use + 1))
                    for k in range(2):
                        last = dve.tensor_scalar(bufa[:, j % 2, k * T:(k + 1) * T],
                                                 bank.tile[:, k * T:(k + 1) * T],
                                                 scale[:, 2 * j + k:2 * j + k + 1],
                                                 shift[:, 2 * j + k:2 * j + k + 1], ALU.mult, ALU.add)
                    last.then_inc(bank.free.sem, 1)
                    dve.wait_ge(norm_hi.sem, norm_hi.at(here, 8 * (which - 1) + j + 1))
                    dve.tensor_tensor(h_lo[:, 2 * j:2 * j + 2, :].rearrange("p k t -> p (k t)"),
                                      bufa[:, j % 2, :],
                                      h_hi[:, 2 * j:2 * j + 2, :].rearrange("p k t -> p (k t)").bitcast(F32),
                                      ALU.subtract).then_inc(h_ready.sem, 1)
                    if j + 2 < 8:
                        stage(j + 2)
                    if j + 1 < 8:
                        split_lo(t0 + (j + 1) // 2, (j + 1) % 2)

            def head_sums(tok, rows, n, scratch):
                dve.tensor_tensor(scratch, rows, rows, ALU.mult).then_inc(dve_step.sem, 1)
                dve.wait_ge(dve_step.sem, step())
                dve.tensor_reduce(ss[0:rows.shape[0], tok, 0:n], scratch.rearrange("p (n d) -> p n d", n=n),
                                  X, ALU.add).then_inc(dve_step.sem, 1)
                dve.wait_ge(dve_step.sem, step())

            def scale_heads(tok, rows, n):
                heads = rows.rearrange("p (n d) -> p n d", n=n)
                part = rows.shape[0]
                dve.tensor_tensor(heads, heads, ss[0:part, tok, 0:n].unsqueeze(2).to_broadcast([part, n, DH]),
                                  ALU.mult).then_inc(stage_ready.sem, 1)

            def stage_sums(c, n):
                for tok in range(TOKS):
                    b = chunk_bank(c, tok)
                    dve.wait_ge(chunk_free[b].sem, chunk_free[b].at(here, c // 2 + 1))
                    head_sums(tok, bufb[:, tok, 0:n * DH], n,
                              pooledT[:].rearrange("p k t -> p (k t)")[:, 0:n * DH])
                rstd(ss[:, :, 0:n], DH)

            def stage_scale(n):
                for tok in range(TOKS):
                    scale_heads(tok, bufb[:, tok, 0:n * DH], n)

            def blocks(i):
                if i == 0:
                    dve.wait_ge(bank_a.free.sem, bank_a.free.at(here, A_USE["kv 0"] + 1))
                    dve.wait_ge(bank_b.free.sem, bank_b.free.at(here, B_USE["kv 0"] + 1))
                src = uc[:, i * 512:(i + 1) * 512].rearrange("p (g c s) -> p g c s", g=KV, s=CMP_STRIDE)
                dst = (bufa, pT)[i][:].rearrange("p a b -> p (a b)")[:, 0:KV * NC * CMP_LEN]\
                    .rearrange("p (g c s) -> p g c s", g=KV, s=CMP_LEN)
                for a in range(2):
                    o = CV["pe"] + i * CMP_LEN + a * CMP_STRIDE
                    pe_cols = cv[:, o:o + CMP_STRIDE].unsqueeze(1).to_broadcast([P, NC, CMP_STRIDE])
                    for g in range(KV):
                        last = dve.tensor_tensor(dst[:, g, :, a * CMP_STRIDE:(a + 1) * CMP_STRIDE],
                                                 src[:, g, a:a + NC, :], pe_cols, ALU.add)
                last.then_inc(blocks_ready.sem, 1)

            def sigmoid_gates():
                for tok in range(TOKS):
                    b = chunk_bank(C_GL, tok)
                    dve.wait_ge(chunk_free[b].sem, chunk_free[b].at(here, C_GL // 2 + 1))
                row = gates[:].rearrange("p q h b -> p (q h b)")
                dve.tensor_scalar(row, row, 1.0, None, ALU.add).then_inc(dve_step.sem, 1)
                dve.wait_ge(dve_step.sem, step())
                dve.reciprocal(row, row).then_inc(dve_step.sem, 1)
                dve.wait_ge(dve_step.sem, step())

            def silu_hidden():
                dve.wait_ge(hid_exp.sem, hid_exp.at(here, 1))
                dve.tensor_scalar(hexp[:], hexp[:], 1.0, None, ALU.add).then_inc(dve_step.sem, 1)
                dve.wait_ge(dve_step.sem, step())
                dve.reciprocal(hexp[:], hexp[:]).then_inc(dve_step.sem, 1)
                dve.wait_ge(dve_step.sem, step())
                dve.tensor_tensor(hid[:], bank_s.tile[:, 0:2 * KV * NC], hexp[:], ALU.mult)\
                    .then_inc(bank_s.free.sem, 1)

            def take_cmp():
                use = S_USE["cmp out"]
                dve.wait_ge(bank_s.full.sem, bank_s.full.at(here, use + 1))
                dve.sem_inc(raw_free[T_CMP2 % 4].sem, 1)
                dve.tensor_copy(vcmp[:].rearrange("p g d -> p (g d)"), bank_s.tile[0:NC, 256:512])
                dve.tensor_copy(bufa[0:NC, 0, 0:256], bank_s.tile[0:NC, 0:256]).then_inc(bank_s.free.sem, 1)
                dve.wait_ge(bank_s.free.sem, bank_s.free.at(here, use + 1))
                head_sums(0, bufa[0:NC, 0, 0:256], KV, pooledT[0:NC, 0, :])
                rstd(ss[0:NC, 0, 0:KV], DH)
                scale_heads(0, bufa[0:NC, 0, 0:256], KV)

            def cmp_bias(g):
                use = S_USE[f"cmp scores {g}"]
                n = TOKS * REP * NC
                row = pc[:, g].rearrange("p n c -> p (n c)")
                dve.wait_ge(bank_s.full.sem, bank_s.full.at(here, use + 1))
                dve.tensor_tensor(row, bank_s.tile[:, 0:n], k_sb[:, K_CMP + g * n:K_CMP + (g + 1) * n], ALU.add)\
                    .then_inc(bank_s.free.sem, 1)
                dve.wait_ge(bank_s.free.sem, bank_s.free.at(here, use + 1))
                dve.tensor_reduce(m8[:], pc[:, g], X, ALU.max, negate=True).then_inc(dve_step.sem, 1)
                dve.wait_ge(dve_step.sem, step())
                dve.tensor_tensor(pc[:, g], pc[:, g], m8[:].unsqueeze(2).to_broadcast([P, 8, NC]), ALU.add)\
                    .then_inc(cmp_biased.sem, 1)

            def cmp_scale(g):
                dve.wait_ge(cmp_exped.sem, cmp_exped.at(here, g + 1))
                dve.tensor_reduce(f8[:], pc[:, g], X, ALU.add).then_inc(dve_step.sem, 1)
                dve.wait_ge(dve_step.sem, step())
                dve.reciprocal(f8[:], f8[:]).then_inc(dve_step.sem, 1)
                dve.wait_ge(dve_step.sem, step())
                f8v = f8[:].rearrange("p (q r) -> p q r", q=TOKS)
                dve.tensor_tensor(f8v, f8v, gates[:, :, REP * g:REP * (g + 1), 0], ALU.mult)\
                    .then_inc(dve_step.sem, 1)
                dve.wait_ge(dve_step.sem, step())
                dve.tensor_scalar(f8[:, 0:REP], f8[:, 0:REP], k_sb[:, K_SEEN:K_SEEN + 1], None, ALU.mult)\
                    .then_inc(dve_step.sem, 1)
                dve.wait_ge(dve_step.sem, step())
                dve.tensor_tensor(pc[:, g], pc[:, g], f8[:].unsqueeze(2).to_broadcast([P, 8, NC]), ALU.mult)\
                    .then_inc(cmp_ready.sem, 1)

            def bias(n):
                u, g, q, h, nk = step_of(n)
                use = S_USE[f"scores {n}"]
                if n >= 2:
                    dve.wait_ge(bank_a.full.sem, bank_a.full.at(here, A_USE[f"probs {n - 2}"] + 1))
                dve.wait_ge(bank_s.full.sem, bank_s.full.at(here, use + 1))
                rows = bufa[:, n % 2, 0:2 * nk].rearrange("p (b k) -> p b k", b=2)
                dist = k_sb[:, K_DIST + 2 * P - nk:K_DIST + 2 * P].unsqueeze(1).to_broadcast([P, 2, nk])
                dve.scalar_tensor_tensor(rows, dist, 2.0 ** -(h + 1),
                                         bank_s.tile[:, 0:2 * nk].rearrange("p (b k) -> p b k", b=2),
                                         ALU.mult, ALU.add).then_inc(bank_s.free.sem, 1)
                dve.wait_ge(bank_s.free.sem, bank_s.free.at(here, use + 1))
                dve.tensor_reduce(nmax[:, n % 2, :], rows, X, ALU.max, negate=True).then_inc(biased.sem, 1)

            def scale(n):
                u, g, q, h, nk = step_of(n)
                dve.wait_ge(exped.sem, exped.at(here, n + 1))
                dve.reciprocal(fac[:], sums[:, n % 2, :]).then_inc(dve_step.sem, 1)
                dve.wait_ge(dve_step.sem, step())
                dve.tensor_tensor(fac[:], fac[:], gates[:, q, h, 1:3], ALU.mult).then_inc(dve_step.sem, 1)
                dve.wait_ge(dve_step.sem, step())
                for b in range(2):
                    row = bufa[:, n % 2, b * nk:(b + 1) * nk]
                    last = dve.tensor_scalar(row, row, fac[:, b:b + 1], None, ALU.mult)
                last.then_inc(p_ready.sem, 1)

            def heads_to_rows(u):
                g, q = u // TOKS, u % TOKS
                dve.wait_ge(heads_hi.sem, heads_hi.at(here, u + 1))
                hi, lo = ((a_hi, a_lo), (h_hi, h_lo))[g]
                r0 = 8 if g == 0 else 0
                dve.tensor_tensor(lo[:, r0:r0 + 4, q * P:(q + 1) * P],
                                  bank_b.tile[:].rearrange("p (r t) -> p r t", r=REP),
                                  hi[:, r0:r0 + 4, q * P:(q + 1) * P].bitcast(F32), ALU.subtract)\
                    .then_inc(bank_b.free.sem, 1)

            def mixed(i):
                dve.wait_ge(mix_hi.sem, mix_hi.at(here, i + 1))
                for d in range(2):
                    k = 2 * i + d
                    last = dve.scalar_tensor_tensor(
                        a_lo[:, k, :], bank_a.tile[:, d * T:(d + 1) * T],
                        cv[:, CV["pool_scale"] + k:CV["pool_scale"] + k + 1],
                        a_hi[:, k, :].bitcast(F32), ALU.mult, ALU.subtract)
                last.then_inc(bank_a.free.sem, 1)

            def into_x(m, t, c, n, buf):
                for tok in range(TOKS):
                    b = chunk_bank(c, tok)
                    dve.wait_ge(gemm_done.sem, gemm_done.at(here, 2 * half_of(t) + 2 + tok + 1))
                    if m > 0:
                        dve.wait_ge(x_updated.sem, x_updated.at(here, 2 * m - 1 + tok))
                    dve.tensor_tensor(buf[:, tok, :], ps[b][:], gate[:, n * 512:(n + 1) * 512], ALU.mult)\
                        .then_inc(chunk_free[b].sem, 1)
                for tok in range(TOKS):
                    b = chunk_bank(c, tok)
                    dve.wait_ge(chunk_free[b].sem, chunk_free[b].at(here, c // 2 + 1))
                    xs = x[:, tok, n * 512:(n + 1) * 512]
                    dve.tensor_tensor(xs, xs, buf[:, tok, :], ALU.add).then_inc(x_updated.sem, 1)

            def conditioning(t):
                for q, at in ADA_REDUCE.items():
                    if t in at and q < 2:
                        take_spread(FIRST_UNITS + q, at.index(t))
                    elif t in at:
                        i = q // 2 - 1
                        bias_at = CV["b_shift2"] + i * KT
                        take_columns(FIRST_UNITS + q, mod2[:, i], cv[:, bias_at:bias_at + KT],
                                     cv[:, CV["g2"]:CV["g2"] + KT])
                for q, at in ADA_PERIODS.items():
                    done = sum(n for tt, n in at.items() if tt < t)
                    for k in range(done, done + at.get(t, 0)):
                        ada_sum(FIRST_UNITS + q, k)

            def period(t, nxt):
                m = PER.index(t) if t in PER else -1
                if 0 <= m < NSTEP:
                    bias(m)
                for u in range(4):
                    if t == PER[4 * u + 5]:
                        heads_to_rows(u)
                if nxt is not None:
                    split_lo(nxt, 0)
                if t == 5:
                    dve.wait_ge(cv_landed.sem, cv_landed.at(here, 16))
                    dve.tensor_scalar(qgs[:], cv[:, CV["q_gain"]:CV["q_gain"] + 1], DH ** -0.5, None, ALU.mult)
                if t == 25:
                    cmp_scale(0)
                if t == 30:
                    cmp_scale(1)
                if 0 <= m < NSTEP:
                    scale(m)
                if nxt is not None:
                    split_lo(nxt, 1)
                if t == 6:
                    blocks(0)
                if t == 7:
                    blocks(1)
                if t == 8:
                    stage_sums(C_KV + 1, 2)
                    stage_scale(2)
                if t == 19:
                    take_cmp()
                if t == 22:
                    stage_sums(C_Q, 4)
                    stage_scale(4)
                if t == 26:
                    stage_sums(C_Q + 1, 4)
                if t == 27:
                    stage_scale(4)
                if t == 24:
                    cmp_bias(0)
                if t == 29:
                    cmp_bias(1)
                for i in range(4):
                    if t == MIX_AT[i]:
                        mixed(i)
                for n in range(4):
                    if t == (38, 40, 42, 44)[n]:
                        into_x(n, T_PASS1[n][1], C_PASS1 + n, n, bufb)
                if t in (46, 48, 50):
                    n = (t - 46) // 2
                    into_x(4 + n, T_PASS2 + 2 * n + 1, C_PASS2 + n, n, bufb)
                conditioning(t)

            def mlp_part(o, ups, groups, last, sums):
                t0, c0 = T_MLP + o * PART_TILES, C_MLP + o * PART_CHUNKS
                tiles = 4 * (ups + groups)

                def times_up(k):
                    if k >= 2:
                        bank, base = (bank_a, A_MLP) if k % 2 == 0 else (bank_b, B_MLP)
                        dve.wait_ge(bank.full.sem, bank.full.at(here, base + 3 * o + (k - 2) // 2 + 1))
                    for tok in range(TOKS):
                        dve.wait_ge(silu_done.sem, silu_done.at(here, 12 * o + 2 * k + tok + 1))
                        b = chunk_bank(c0 + k, tok)
                        dve.tensor_tensor(bufb[:, k % 2, tok * 256:(tok + 1) * 256],
                                          bufa[:, k % 2, tok * 256:(tok + 1) * 256], ps[b][:, 256:512],
                                          ALU.mult).then_inc(chunk_free[b].sem, 1)

                def rows(k):
                    bank = bank_a if k % 2 == 0 else bank_b
                    dve.wait_ge(ff_hi.sem, ff_hi.at(here, 6 * o + k + 1))
                    hi = a_hi[:, 2 * k:2 * k + 2, :].rearrange("p k t -> p (k t)").bitcast(F32)
                    dve.tensor_tensor(a_lo[:, 2 * k:2 * k + 2, :].rearrange("p k t -> p (k t)"), bank.tile[:],
                                      hi, ALU.subtract).then_inc(bank.free.sem, 1)

                def down(n):
                    into_x(8 + 4 * o + n, t0 + 4 * ups + groups * (n + 1) - 1, c0 + ups + n, n, bufa)

                for m in range(3 if o == 0 else 0, tiles):
                    k = m // 4 - 1
                    if m % 4 == 0 and 0 <= k < ups:
                        times_up(k)
                    n, g = divmod(m - 4 * ups, groups)
                    if m >= 4 * ups and g == 0 and n >= 1:
                        down(n - 1)
                    if not (last and m == tiles - 1):
                        split_lo(t0 + m + 1, 0)
                        split_lo(t0 + m + 1, 1)
                    if m % 4 == 0 and 0 <= k < ups:
                        rows(k)
                    sums(m)
                down(3)

            def gate2_sums(m):
                for i, (first, counts) in enumerate(PART_ADA):
                    if m in PART_REDUCE[i]:
                        take_spread(FIRST_UNITS + 6 + i, PART_REDUCE[i].index(m))
                    if first <= m < first + len(counts):
                        done = sum(counts[:m - first])
                        for k in range(done, done + counts[m - first]):
                            ada_sum(FIRST_UNITS + 6 + i, k)

            def next_sums(m):
                for i, (first, counts) in enumerate(PART_ADA):
                    if m != PART_REDUCE[i][0] and not first <= m < first + len(counts):
                        continue
                    with dve.If(here.layer < DEPTH - 1):
                        if m == PART_REDUCE[i][0]:
                            if i == 0:
                                dve.wait_ge(nv_landed.sem, nv_landed.at(here, 16))
                            table = mod1[:, bass.ds(here.part, 1)].rearrange("p o a k -> p (o a) k")
                            b = nv[:, bass.ds(here.part * KT + KT, KT)]
                            take_columns(FIRST_UNITS + 8 + i, table, b, nv[:, 0:KT])
                        if first <= m < first + len(counts):
                            done = sum(counts[:m - first])
                            for k in range(done, done + counts[m - first]):
                                ada_sum(FIRST_UNITS + 8 + i, k)

            dve.sem_inc(acc_step.sem, 4)
            dve.wait_ge(cond_ready.sem, 17)
            dve.wait_ge(first_landed.sem, 32)
            for q in range(FIRST_UNITS):
                for k in range(KT):
                    ada_sum(q, k)
                take_columns(q, mod1[:, q // 2], nv[:, KT * (1 + q // 2):KT * (2 + q // 2)], nv[:, 0:KT])

            with dve.Fori(0, DEPTH) as layer:
                here.layer = layer
                norm(1, 0, (mod1[:, 0, 0], mod1[:, 1, 1]))
                for t in range(3, 12):
                    period(t, t + 1 if t < 11 else None)
                stage_sums(C_KV + 2, 2)
                stage_scale(2)
                conditioning(12)
                sigmoid_gates()
                silu_hidden()
                split_lo(T_Q, 0)
                split_lo(T_Q, 1)
                split_tiles = [t for t in range(T_Q, T_MLP) if t not in DIRECT]
                for i, t in enumerate(split_tiles):
                    period(t, split_tiles[i + 1] if i + 1 < len(split_tiles) else None)
                into_x(7, T_PASS2 + 7, C_PASS2 + 3, 3, bufb)
                norm(2, T_MLP, (mod2[:, 0, 0], mod2[:, 1, 1]))
                for m in range(3):
                    gate2_sums(m)
                mlp_part(0, PART_UP, PART_G, False, gate2_sums)
                with dve.Fori(0, PARTS - 1) as part:
                    here.part = part
                    mlp_part(1, PART_UP, PART_G, False, next_sums)
                here.part = None
                mlp_part(PARTS, LAST_UP, LAST_G, True, lambda m: None)
            assert steps[0] == DVE_STEPS, steps


def layer_stream(w_in, w_cmp1, w_cmp2, w_pool, w_out, w_gate_up, w_down, pool_m):
    out = np.zeros((TILES, P, 4 * COLS), np.float32)
    place = iter([t for t in range(TILES) if t not in DIRECT])

    def put(w, kts, cols):
        block = w.reshape(-1, P, w.shape[1])
        out[next(place)].reshape(P, 4, COLS)[:] = block[kts][:, :, cols].transpose(1, 0, 2)

    def chunk(w, first, kts):
        for g in range(0, len(kts), 4):
            put(w, kts[g:g + 4], np.arange(first, first + COLS))

    every = list(range(KT))
    for first in (2048, 2560, 3072, 1024, 1536, 0, 512):
        chunk(w_in, first, every)
    out[T_GL][:, :384] = w_in[:, 3584:].reshape(KT, P, 24).transpose(1, 0, 2).reshape(P, 384)
    for i in range(2):
        w = w_cmp1[i].reshape(2, 16, P, P).transpose(0, 2, 1, 3)
        for a in range(2):
            out[T_CMP1 + 2 * i + a] = w[a].reshape(P, 16 * P)
    out[T_CMP2][:, :256] = w_cmp2.transpose(1, 0, 2).reshape(P, 256)
    for i, t in enumerate(T_POOL):
        out[t][:, :768] = pool_m[:, 2 * i:2 * i + 2].reshape(P, 768)
        w = w_pool[2 * i:2 * i + 2].reshape(2, 2, P, PG).transpose(2, 0, 1, 3)
        out[t][:, 768:1792] = w.reshape(P, 1024)
    for kts in ([0, 1, 2, 3, 8, 9, 10, 11], [4, 5, 6, 7, 12, 13, 14, 15]):
        for n in range(4):
            chunk(w_out, n * COLS, kts)
    for part in range(PARTS + 1):
        ups = PART_UP if part < PARTS else LAST_UP
        first = part * PART_KT
        for k in range(ups):
            f = first * P + k * FCH
            for g in range(4):
                put(w_gate_up, every[4 * g:4 * g + 4],
                    np.concatenate([np.arange(f, f + FCH), np.arange(FF + f, FF + f + FCH)]))
        for n in range(4):
            chunk(w_down, n * COLS, list(range(first, first + 2 * ups)))
    assert next(place, None) is None
    return out


def kernel(x, c, w_ada, b_ada, norm_g, w_in, q_gain, k_gain, pe_cmp, w_cmp1, w_cmp2, w_pool, pool_scale,
           w_out, w_gate_up, w_down):
    import concourse.bacc as bacc
    from concourse.bass_utils import run_bass_kernel_spmd

    f = {k: np.ascontiguousarray(v) for k, v in dict(
        x=x, c=c, w_ada=w_ada, b_ada=b_ada, norm_g=norm_g, w_in=w_in, q_gain=q_gain, k_gain=k_gain,
        pe_cmp=pe_cmp, w_cmp1=w_cmp1, w_cmp2=w_cmp2, w_pool=w_pool, pool_scale=pool_scale, w_out=w_out,
        w_gate_up=w_gate_up, w_down=w_down).items()}
    pool_m = pool_matrices()
    stream = np.stack([layer_stream(*[f[n][l] for n in ("w_in", "w_cmp1", "w_cmp2", "w_pool", "w_out",
                                                        "w_gate_up", "w_down")], pool_m)
                       for l in range(DEPTH)])
    b = f["b_ada"].reshape(DEPTH, 6, KT, P)
    gain = f["norm_g"].reshape(DEPTH, 2, KT, P)

    def columns(*vectors):
        return np.concatenate([v.reshape(-1, P) for v in vectors]).T

    vec = np.stack([columns(gain[l, 1], b[l, 3], b[l, 4], f["pool_scale"][l], f["q_gain"][l], f["k_gain"][l],
                            f["pe_cmp"][l]) for l in range(DEPTH)])
    vec_next = np.stack([columns(gain[l, 0], b[l, 0], b[l, 1]) for l in range(DEPTH)]
                        + [np.zeros((P, NV_N), np.float32)])
    arrays = {"x": f["x"].reshape(T, D), "stream": stream, "w_ada": f["w_ada"], "b_ada": f["b_ada"],
              "vec": np.ascontiguousarray(vec), "vec_next": np.ascontiguousarray(vec_next),
              "c_col": np.ascontiguousarray(columns(f["c"])), "const": constants()}
    nc = bacc.Bacc("TRN2", target_bir_lowering=False, num_devices=1)
    args = [nc.dram_tensor(n, a.shape, mybir.dt.from_np(a.dtype), kind="ExternalInput").ap()
            for n, a in arrays.items()]
    out = nc.dram_tensor("out", (T, D), F32, kind="ExternalOutput").ap()
    build(nc, *args, out)
    r = run_bass_kernel_spmd(nc, [arrays], core_ids=[0])
    return r.results[0]["out"].reshape(1, T, D)
```

```python
from contextlib import ExitStack

import numpy as np

import concourse.bass as bass
from concourse import mybir

ALU = mybir.AluOpType
ACT = mybir.ActivationFunctionType
F32 = mybir.dt.float32
F32R = mybir.dt.float32r
I32 = mybir.dt.int32
X = mybir.AxisListType.X

P = 128
D, T, DEPTH = 2048, 256, 2
TOKS = T // P
KT = D // P
POOL, HEADS, KV, DH = 1024, 8, 2, 128
REP = HEADS // KV
POOL_WINDOWS = (2, 4, 8, 16)
PG = POOL // len(POOL_WINDOWS)
CMP_LEN, CMP_STRIDE = 32, 16
NC = (T - CMP_LEN) // CMP_STRIDE + 1
FF = 5632
EPS = 1e-6
NEG = -1e30
COLS = 512
FCH = 256

DVE_STEPS = 126

T_KV, T_GL, T_CMP1, T_CMP2 = 0, 12, 13, 17
T_Q, T_U0, T_POOL, T_PASS2, T_MLP = 18, 26, (32, 37), 44, 52
T_U1 = (30, 31, 33, 34)
T_PASS1 = ((35, 36), (38, 39), (40, 41), (42, 43))
DIRECT = (12, 13, 14, 15, 16, 17, 32, 37)
PART_KT = 12
PARTS = 3
LAST_KT = FF // P - PARTS * PART_KT
PART_UP, LAST_UP = PART_KT // 2, LAST_KT // 2
PART_G, LAST_G = PART_KT // 4, LAST_KT // 4
PART_TILES = 4 * PART_UP + 4 * PART_G
LAST_TILES = 4 * LAST_UP + 4 * LAST_G
TILES = T_MLP + PARTS * PART_TILES + LAST_TILES
assert TILES % 4 == 0 and PART_TILES % 4 == 0 and FF % (2 * FCH) == 0


def half_of(t):
    return 2 * (t - sum(d < t for d in DIRECT))


HALVES = half_of(TILES)
PART_HALVES = 2 * PART_TILES
assert HALVES % 4 == 0

C_KV, C_GL, C_Q, C_U, C_PASS1, C_PASS2, C_MLP = 0, 3, 4, 6, 8, 12, 16
PART_CHUNKS = PART_UP + 4
CHUNKS = C_MLP + PARTS * PART_CHUNKS + LAST_UP + 4
assert CHUNKS % 2 == 0 and PART_CHUNKS % 2 == 0

STEP_PERIODS = (25, 26, 27, 28, 29, 30, 31, 33, 34, 35, 36, 38, 39, 40, 41, 42, 43, 44)
NSTEP = 16
SIDE, MID = 0, 1
POOLED_AT = (31, 33, 36, 38)
MIX_AT = (33, 34, 38, 39)


def done_before(o, ups, m):
    if o == 0 and m in (4, 7):
        return [0] if m == 7 else []
    return [m // 4 - 1] if m % 4 == 0 and 1 <= m // 4 <= ups else []


def turned_at(o, ups, m):
    return [] if o == 0 and m == 7 else [0, 1] if o == 0 and m == 8 else done_before(o, ups, m)


def ordered(events):
    return {name: i for i, (_, _, name) in enumerate(sorted(events, key=lambda e: e[:2]))}


S_USE = ordered(
    [(12, 0, "hidden"), (19, SIDE, "hidden turned"), (19, MID, "cmp out"), (24, MID, "cmp scores 0"),
     (28, MID, "q 1"), (29, MID, "cmp scores 1")]
    + [(STEP_PERIODS[n], SIDE, f"scores {n}") for n in range(NSTEP)]
    + [(STEP_PERIODS[4 * u + 1], MID, f"cmp probs {u}") for u in range(4)]
    + [(POOLED_AT[i], MID, f"pooled {i}") for i in range(4)])
A_USE = ordered(
    [(-9 + j, 0, f"norm1 {j}") for j in range(0, 8, 2)]
    + [(8, SIDE, "kv 0"), (10, SIDE, "kv 1"), (13, SIDE, "kv 2"), (22, SIDE, "kcmp"), (24, SIDE, "q 0"),
       (28, MID, "q 1")]
    + [(STEP_PERIODS[n + 1], SIDE, f"probs {n}") for n in range(NSTEP)]
    + [(MIX_AT[i], MID, f"mix {i}") for i in range(4)]
    + [(50 + j, 0, f"norm2 {j}") for j in range(0, 8, 2)])
B_USE = ordered(
    [(-9 + j, 0, f"norm1 {j}") for j in range(1, 8, 2)]
    + [(8, SIDE, "kv 0"), (10, SIDE, "kv 1"), (13, SIDE, "kv 2"), (24, SIDE, "q 0")]
    + [(STEP_PERIODS[4 * u + 2], SIDE, f"heads {u}") for u in range(4)]
    + [(50 + j, 0, f"norm2 {j}") for j in range(1, 8, 2)])
A_MLP, B_MLP = len(A_USE), len(B_USE)

ST_NORM1, ST_KV, ST_KCMP, ST_Q, ST_NORM2, STAGES = 0, 8, 12, 13, 17, 25

assert DEPTH == 2


class Unit:

    def __init__(self, first, per_layer=0, per_part=0):
        self.first, self.per_layer, self.per_part = first, per_layer, per_part

    def at(self, here, each, n):
        return here.value(each * self.first + n, each * self.per_layer, each * self.per_part)


FIRST_UNITS = 4
GATE1 = [Unit(4 + i, 16) for i in range(2)]
FIRST_MOD2 = [Unit(6 + i) for i in range(4)]
GATE2 = [Unit(10 + i, 12) for i in range(2)]
LOOP_UNITS = 3
NEXT_LOOP = [Unit(12 + i, 12, LOOP_UNITS) for i in range(LOOP_UNITS)]
NEXT_LAST = [Unit(12 + LOOP_UNITS * (PARTS - 1) + i, 12) for i in range(8 - LOOP_UNITS * (PARTS - 1))]
UNITS = 12 * DEPTH


def schedule(room, reduces):
    sums, reductions, periods, i = [], [], sorted(room), 0
    for n, slack in reduces:
        left, mine = KT, {}
        while left:
            mine[periods[i]] = min(left, room[periods[i]])
            left -= mine[periods[i]]
            i += 1
        sums.append(mine)
        reductions.append(tuple(periods[i + slack:i + slack + n]))
        assert len(reductions[-1]) == n, "no room"
        i += slack + n - 1
    return sums, reductions


ROOM = {7: 3, 8: 3, 9: 3, 10: 3, 11: 4, 12: 4, 13: 6, 14: 2, 18: 3, 19: 1, 20: 4, 21: 3, 22: 1, 23: 3} \
    | {t: 3 for t in range(24, T_MLP) if t not in DIRECT} | {26: 1, 27: 2}
ADA_SUMS, ADA_REDUCE = schedule(ROOM, ((2, 0), (2, 0), (1, 1), (1, 1), (1, 0), (1, 0)))
GATE2_SUMS, GATE2_REDUCE = schedule({m: 2 for m in range(7, 27)}, ((2, 0), (2, 0)))
LOOP_SUMS, LOOP_REDUCE = schedule({m: 1 + (m % 3 != 2) for m in range(PART_TILES)}, ((1, 1),) * LOOP_UNITS)
LAST_SUMS, LAST_REDUCE = schedule({m: 2 for m in range(LAST_TILES)}, ((1, 1),) * len(NEXT_LAST))

CV = {"pool_scale": 0, "q_gain": 8, "k_gain": 9, "pe": 12}
CV_N = 76
NV_BIAS, NV_GAIN, NV_N = 0, 64, 128
K_ID, K_ONE, K_DIST, K_CMP, K_SEEN = 0, 128, 256, 512, 512 + 2 * 8 * NC
K_N = K_SEEN + 1


def constants():
    k = np.zeros((P, K_N), np.float32)
    k[:, K_ID:K_ID + P] = np.eye(P)
    k[:, K_ONE:K_ONE + P] = 1.0
    t, j = np.arange(P)[:, None], np.arange(P)[None, :]
    k[:, K_DIST:K_DIST + P] = -(P + t - j)
    k[:, K_DIST + P:K_DIST + 2 * P] = np.where(t >= j, -(t - j), -1e33)
    end = np.arange(NC) * CMP_STRIDE + CMP_LEN - 1
    cmp = k[:, K_CMP:K_SEEN].reshape(P, KV, TOKS, REP, NC)
    for g in range(KV):
        for q in range(TOKS):
            for r in range(REP):
                dist = q * P + t - end[None, :]
                cmp[:, g, q, r] = np.where(dist >= 0, -(2.0 ** -(g * REP + r + 1)) * dist, NEG)
    k[:, K_SEEN] = np.arange(P) >= end[0]
    return k


def pool_matrices():
    out = np.zeros((P, len(POOL_WINDOWS), 3 * P), np.float32)
    t = np.arange(T)
    for i, w in enumerate(POOL_WINDOWS):
        count = np.minimum(t + 1, w)
        m = np.where((t[:, None] <= t[None, :]) & (t[:, None] > t[None, :] - w), 1.0 / count[None, :], 0.0)
        m = m - np.eye(T)
        out[:, i, :T] = m[:P]
        out[:, i, T:] = m[P:, P:]
    return out


class Place:

    def __init__(self):
        self.layer = self.part = None

    def value(self, n, per_layer, per_part=0):
        if self.part is not None and per_part:
            n = self.part * per_part + n
        if self.layer is not None:
            n = self.layer * per_layer + n
        return n


class Count:

    def __init__(self, sem, per_layer, per_part=0, start=0):
        self.sem, self.per_layer, self.per_part, self.start = sem, per_layer, per_part, start

    def at(self, here, n):
        return here.value(n + self.start, self.per_layer, self.per_part)


class Bank:

    def __init__(self, tile, full, free):
        self.tile, self.full, self.free = tile, full, free


def build(nc, x_in, stream, w_ada, b_ada, vec, vec_next, c_col, const, out):
    ctx = ExitStack()
    with ctx:
        def sb(name, shape, dt=F32):
            return ctx.enter_context(nc.sbuf_tensor(name, shape, dt))

        def count(name, per_layer=0, per_part=0, start=0):
            return Count(ctx.enter_context(nc.semaphore(name)), per_layer, per_part, start)

        raw = [sb(f"raw{s}", [P, 4 * COLS]) for s in range(4)]
        whi = [sb(f"w_hi{s}", [P, 2, COLS], F32R) for s in range(4)]
        wlo = [sb(f"w_lo{s}", [P, 2, COLS], F32R) for s in range(4)]
        x = sb("x_sb", [P, TOKS, D])
        h_hi, h_lo = sb("h_hi", [P, KT, T], F32R), sb("h_lo", [P, KT, T], F32R)
        a_hi, a_lo = sb("a_hi", [P, PART_KT, T], F32R), sb("a_lo", [P, PART_KT, T], F32R)
        ada = [sb(f"ada{s}", [P, 1024]) for s in range(4)]
        acc = sb("acc", [P, 1024])
        gate = sb("gate", [P, D])
        cond = sb("cond", [P, KT])
        ccol = sb("ccol", [P, KT])
        cv, nv = sb("cv", [P, CV_N]), sb("nv", [P, NV_N])
        mod = sb("mod", [P, 8, 2, 8])
        k_sb = sb("k_sb", [P, K_N])
        bufa = sb("bufa", [P, 2, 512])
        bufb = sb("bufb", [P, 2, 512])
        uc = sb("uc", [P, 1024])
        kT = sb("kT", [P, 2, KV, T])
        val = sb("val", [P, TOKS, 2, KV * DH])
        qT = sb("qT", [P, TOKS, HEADS, P])
        pT = sb("pT", [P, 2, 512])
        pooledT = sb("pooledT", [P, 2, T])
        pcT = sb("pcT", [NC, REP * P])
        kcT = sb("kcT", [P, KV, 16])
        vcmp = sb("vcmp", [NC, KV, DH])
        hid = sb("hid", [P, 2, KV * NC])
        pc = sb("pc", [P, KV, TOKS * REP, NC])
        gates = sb("gates", [P, TOKS, HEADS, 3])
        qgs = sb("qgs", [P, 1])
        ssq, rs = sb("ssq", [P, TOKS, 4]), sb("rs", [P, TOKS])
        ss = sb("ss", [P, TOKS, 4])
        root, root_err = sb("root", [P, 8]), sb("root_err", [P, 8])
        m8, f8 = sb("m8", [P, 8]), sb("f8", [P, 8])
        nmax, sums, fac = sb("nmax", [P, 2, 2]), sb("sums", [P, 2, 2]), sb("fac", [P, 2])

        ident = k_sb[:, K_ID:K_ID + P]
        ones = k_sb[:, K_ONE:K_ONE + P]
        gate_w = [part[:].rearrange("p k t -> p (k t)")[:, 0:24 * KT] for part in (a_hi, a_lo)]

        ps = [ctx.enter_context(nc.psum_tensor(f"ps{b}", [P, 512], F32)) for b in range(8)]
        mod_ps = ps[7]

        a_uses, b_uses = A_MLP + PARTS * 3 + 2, B_MLP + PARTS * 3 + 2
        bank_s = Bank(ps[4], count("s_full", len(S_USE)), count("s_free", len(S_USE), 0, 1))
        bank_a = Bank(ps[5], count("a_full", a_uses, 3), count("a_free", a_uses, 3, 1))
        bank_b = Bank(ps[6], count("b_full", b_uses, 3), count("b_free", b_uses, 3, 1))
        raw_landed = [count(f"raw_landed{s}", 4 * TILES, 4 * PART_TILES) for s in range(4)]
        raw_free = [count(f"raw_free{s}", TILES // 4, PART_TILES // 4) for s in range(4)]
        ada_landed = [count(f"ada_landed{s}") for s in range(4)]
        first_landed = count("first_landed")
        x_landed = count("x_landed")
        cv_landed, nv_landed = count("cv_landed", 16), count("nv_landed", 16)
        gate_landed = count("gate_landed", 32)
        hi_ready = count("hi_ready", HALVES, PART_HALVES)
        lo_ready = count("lo_ready", HALVES, PART_HALVES)
        gemm_done = count("gemm_done", 2 * HALVES, 2 * PART_HALVES, 8)
        chunk_free = [count(f"chunk_free{b}", CHUNKS // 2, PART_CHUNKS // 2, 1) for b in range(4)]
        stage_ready = count("stage_ready", STAGES)
        norm_hi, h_ready = count("norm_hi", 16), count("h_ready", 16)
        x_updated = count("x_updated", 16 + 8 * PARTS + 8, 8)
        squared = count("squared", 16, 0, 8)
        silu_done = count("silu_done", 12 * PARTS + 2 * LAST_UP, 12)
        ff_hi = count("ff_hi", 6 * PARTS + LAST_UP, 6)
        cond_ready = count("cond_ready")
        acc_step = count("acc_step", start=4)
        acc_summed = count("acc_summed")
        mod_free = count("mod_free", start=1)
        blocks_ready = count("blocks_ready", 2)
        gl_hi, gl_lo = count("gl_hi", 1), count("gl_lo", 1)
        gl_done, gl_turned = count("gl_done", 1), count("gl_turned", 1)
        hid_exp = count("hid_exp", 1)
        biased, exped, p_ready = count("biased", NSTEP), count("exped", NSTEP), count("p_ready", NSTEP)
        cmp_biased, cmp_exped, cmp_ready = count("cmp_biased", 2), count("cmp_exped", 2), count("cmp_ready", 2)
        mix_hi, heads_hi = count("mix_hi", 4), count("heads_hi", 4)
        dve_step = count("dve_step", DVE_STEPS)
        stored = count("stored")

        def chunk_bank(c, tok):
            return 2 * (c % 2) + tok

        def step_of(n):
            u = n // REP
            g, q = u // TOKS, u % TOKS
            return u, g, q, g * REP + n % REP, (q + 1) * P

        block = ctx.enter_context(nc.Block())

        @block.sync
        def _(sp):
            sp.dma_start(k_sb[:], const).then_inc(first_landed.sem, 16)
            sp.dma_start(nv[:], vec_next[0]).then_inc(first_landed.sem, 16)
            sp.dma_start(x[:], x_in.rearrange("(q p) d -> p q d", p=P)).then_inc(x_landed.sem, 16)
            flat = stream.rearrange("l t p c -> (l t) p c")
            for s in range(4):
                if s == 1:
                    sp.wait_ge(acc_step.sem, 4 + 16 * FIRST_UNITS - 1)
                sp.dma_start(raw[s][:], flat[s]).then_inc(raw_landed[s].sem, 16)
            with sp.Fori(1, DEPTH * TILES // 4) as i:
                for s in range(4):
                    sp.wait_ge(raw_free[s].sem, i)
                    sp.dma_start(raw[s][:], flat[bass.ds(4 * i + s, 1)].rearrange("o p c -> (o p) c"))\
                        .then_inc(raw_landed[s].sem, 16)
            rows = out.rearrange("(q p) d -> p q d", p=P)
            for n in range(4):
                sp.wait_ge(x_updated.sem, DEPTH * x_updated.per_layer - 8 + 2 * (n + 1))
                sp.dma_start(rows[:, :, n * 512:(n + 1) * 512], x[:, :, n * 512:(n + 1) * 512])\
                    .then_inc(stored.sem, 16)
            sp.wait_ge(stored.sem, 64)

        @block.gpsimd
        def _(pool):
            with pool.Fori(0, UNITS) as u:
                for k in range(KT):
                    pool.wait_ge(acc_step.sem, u * 16 + (k + 1))
                    pool.dma_start(ada[k % 4][:], w_ada[bass.ds(u, 1), k].rearrange("o p n -> (o p) n"))\
                        .then_inc(ada_landed[k % 4].sem, 16)

        @block.tensor
        def _(pe):
            here = Place()

            def tile(t, c, rows, first, last, between=None):
                h = half_of(t)
                for a in range(2):
                    s = (h + a) % 4
                    pe.wait_ge(hi_ready.sem, hi_ready.at(here, h + a + 1))
                    pe.wait_ge(lo_ready.sem, lo_ready.at(here, h + a + 1))
                    for tok in range(TOKS):
                        b = chunk_bank(c, tok)
                        if first and a == 0:
                            pe.wait_ge(chunk_free[b].sem, chunk_free[b].at(here, c // 2))
                        for k in range(2):
                            xh, xl = rows[2 * a + k]
                            xh, xl = xh[:, tok * P:(tok + 1) * P], xl[:, tok * P:(tok + 1) * P]
                            begin = first and a == 0 and k == 0
                            end = last and a == 1 and k == 1
                            mm = pe.matmul(ps[b][:], xh, whi[s][:, k, :], start=begin, stop=False)
                            if a == 1 and tok == 0 and k == 0:
                                mm.then_inc(raw_free[t % 4].sem, 1)
                            pe.matmul(ps[b][:], xh, wlo[s][:, k, :], start=False, stop=False)
                            mm = pe.matmul(ps[b][:], xl, whi[s][:, k, :], start=False, stop=end)
                        mm.then_inc(gemm_done.sem, 1)
                    if a == 0 and between is not None:
                        between()

            def h_rows(g):
                return [(h_hi[:, 4 * g + i, :], h_lo[:, 4 * g + i, :]) for i in range(4)]

            def a_rows(g):
                return [(a_hi[:, 4 * g + i, :], a_lo[:, 4 * g + i, :]) for i in range(4)]

            def loaded(t):
                pe.wait_ge(raw_landed[t % 4].sem, raw_landed[t % 4].at(here, 16 * (t // 4 + 1)))

            def norm_turn(which, j):
                bank, uses = (bank_a, A_USE) if j % 2 == 0 else (bank_b, B_USE)
                pe.wait_ge(bank.free.sem, bank.free.at(here, uses[f"norm{which} {j}"]))
                pe.wait_ge(stage_ready.sem, stage_ready.at(here, (ST_NORM1 if which == 1 else ST_NORM2) + j + 1))
                for k in range(2):
                    for tok in range(TOKS):
                        o = (k * TOKS + tok) * P
                        mm = pe.transpose(bank.tile[:, o:o + P],
                                          bufb[:, j % 2, tok * 256 + k * P:tok * 256 + (k + 1) * P], ident)
                mm.then_inc(bank.full.sem, 1)

            def norm(which, t0, c):
                split = 8 * (which - 1)
                norm_turn(which, 0)
                norm_turn(which, 1)
                for g in range(4):
                    for i in range(2):
                        def between(g=g, i=i):
                            if i == 0:
                                pe.wait_ge(h_ready.sem, h_ready.at(here, split + 2 * g + 2))
                        if g < 3:
                            norm_turn(which, 2 * g + 2 + i)
                        if i == 0:
                            pe.wait_ge(h_ready.sem, h_ready.at(here, split + 2 * g + 1))
                        tile(t0 + 2 * g + i, c + i, h_rows(g), g == 0, g == 3, between)

            def stage_turn(bank, use, st, tok, n, stage=None):
                stage = bufb[:, tok] if stage is None else stage
                pe.wait_ge(bank.free.sem, bank.free.at(here, use))
                if st is not None:
                    pe.wait_ge(stage_ready.sem, stage_ready.at(here, st + 1))
                for i in range(n):
                    mm = pe.transpose(bank.tile[:, i * P:(i + 1) * P], stage[:, i * P:(i + 1) * P], ident)
                mm.then_inc(bank.full.sem, 1)

            def gate_logits():
                pe.wait_ge(gl_lo.sem, gl_lo.at(here, 1))
                b = chunk_bank(C_GL, 0)
                pe.wait_ge(chunk_free[b].sem, chunk_free[b].at(here, C_GL // 2))
                for k in range(KT):
                    for i, (w, h) in enumerate(((0, h_hi), (1, h_hi), (0, h_lo))):
                        mm = pe.matmul(ps[b][0:24, 0:T], gate_w[w][:, 24 * k:24 * (k + 1)], h[:, k, :],
                                       start=(k == 0 and i == 0), stop=(k == KT - 1 and i == 2))
                        if k == 0 and i == 0:
                            mm.then_inc(raw_free[T_GL % 4].sem, 1)
                mm.then_inc(gl_done.sem, 1)

            def gates_turn():
                b = chunk_bank(C_GL, 0)
                pe.wait_ge(chunk_free[b].sem, chunk_free[b].at(here, C_GL // 2 + 1))
                b = chunk_bank(C_GL, 1)
                pe.wait_ge(chunk_free[b].sem, chunk_free[b].at(here, C_GL // 2))
                for tok in range(TOKS):
                    mm = pe.transpose(ps[b][:, tok * P:(tok + 1) * P], uc[:, (2 + tok) * P:(3 + tok) * P], ident)
                mm.then_inc(gl_turned.sem, 1)

            def hidden(i):
                if i == 0:
                    pe.wait_ge(bank_s.free.sem, bank_s.free.at(here, S_USE["hidden"]))
                pe.wait_ge(blocks_ready.sem, blocks_ready.at(here, i + 1))
                blk = (bufa, pT)[i][:].rearrange("p a b -> p (a b)")[:, 0:KV * NC * CMP_LEN]\
                    .rearrange("p (n s) -> p n s", s=CMP_LEN)
                for pos in range(CMP_LEN):
                    t = T_CMP1 + 2 * i + pos // 16
                    if pos % 16 == 0:
                        loaded(t)
                    mm = pe.matmul(bank_s.tile[0:KV * NC, i * P:(i + 1) * P], blk[:, :, pos],
                                   raw[t % 4][:, (pos % 16) * P:(pos % 16 + 1) * P],
                                   start=(pos == 0), stop=(pos == CMP_LEN - 1))
                    if pos == 15 or (pos == 31 and i == 0):
                        mm.then_inc(raw_free[t % 4].sem, 1)
                if i == 1:
                    mm.then_inc(bank_s.full.sem, 1)

            def hidden_turn():
                pe.wait_ge(bank_s.free.sem, bank_s.free.at(here, S_USE["hidden turned"]))
                for i in range(2):
                    mm = pe.transpose(bank_s.tile[:, i * P:(i + 1) * P], bufa[:, 0, i * P:(i + 1) * P], ident)
                mm.then_inc(bank_s.full.sem, 1)

            def cmp_out():
                pe.wait_ge(bank_s.free.sem, bank_s.free.at(here, S_USE["cmp out"]))
                pe.wait_ge(bank_s.free.sem, bank_s.free.at(here, S_USE["hidden turned"] + 1))
                loaded(T_CMP2)
                for i in range(2):
                    for g in range(KV):
                        o = (i * KV + g) * DH
                        mm = pe.matmul(bank_s.tile[0:NC, o:o + DH],
                                       hid[:, i, g * NC:(g + 1) * NC],
                                       raw[T_CMP2 % 4][:, i * DH:(i + 1) * DH], start=True, stop=True)
                mm.then_inc(bank_s.full.sem, 1)

            def kcmp_turn():
                pe.wait_ge(bank_a.free.sem, bank_a.free.at(here, A_USE["kcmp"]))
                pe.wait_ge(stage_ready.sem, stage_ready.at(here, ST_KCMP + 1))
                for g in range(KV):
                    mm = pe.transpose(bank_a.tile[:, g * P:(g + 1) * P], bufa[:, 0, g * DH:(g + 1) * DH], ident)
                mm.then_inc(bank_a.full.sem, 1)

            def cmp_scores(g):
                pe.wait_ge(bank_s.free.sem, bank_s.free.at(here, S_USE[f"cmp scores {g}"]))
                pe.wait_ge(bank_a.free.sem, bank_a.free.at(here, A_USE["kcmp"] + 1))
                pe.wait_ge(bank_a.free.sem, bank_a.free.at(here, A_USE[f"q {g}"] + 1))
                if g == 0:
                    pe.wait_ge(bank_b.free.sem, bank_b.free.at(here, B_USE["q 0"] + 1))
                else:
                    pe.wait_ge(bank_s.free.sem, bank_s.free.at(here, S_USE["q 1"] + 1))
                for q in range(TOKS):
                    for r in range(REP):
                        o = (q * REP + r) * NC
                        mm = pe.matmul(bank_s.tile[:, o:o + NC], qT[:, q, g * REP + r, :], kcT[:, g, 0:NC],
                                       start=True, stop=True)
                mm.then_inc(bank_s.full.sem, 1)

            def scores(n):
                u, g, q, h, nk = step_of(n)
                pe.wait_ge(bank_s.free.sem, bank_s.free.at(here, S_USE[f"scores {n}"]))
                if n == 0:
                    pe.wait_ge(bank_a.free.sem, bank_a.free.at(here, A_USE["kv 2"] + 1))
                    pe.wait_ge(bank_b.free.sem, bank_b.free.at(here, B_USE["kv 2"] + 1))
                pe.matmul(bank_s.tile[:, 0:2 * nk], qT[:, q, h, :], kT[:, :, g, 0:nk], start=True,
                          stop=True).then_inc(bank_s.full.sem, 1)

            def probs_turn(n):
                u, g, q, h, nk = step_of(n)
                pe.wait_ge(bank_a.free.sem, bank_a.free.at(here, A_USE[f"probs {n}"]))
                pe.wait_ge(p_ready.sem, p_ready.at(here, n + 1))
                for i in range(2 * nk // P):
                    mm = pe.transpose(bank_a.tile[:, i * P:(i + 1) * P], bufa[:, n % 2, i * P:(i + 1) * P],
                                      ident)
                mm.then_inc(bank_a.full.sem, 1)

            def cmp_probs_turn(u):
                g, q = u // TOKS, u % TOKS
                pe.wait_ge(bank_s.free.sem, bank_s.free.at(here, S_USE[f"cmp probs {u}"]))
                pe.wait_ge(cmp_ready.sem, cmp_ready.at(here, g + 1))
                for r in range(REP):
                    mm = pe.transpose(bank_s.tile[0:NC, r * P:(r + 1) * P], pc[:, g, q * REP + r, :], ident)
                mm.then_inc(bank_s.full.sem, 1)

            def head_out(n):
                u, g, q, h, nk = step_of(n)
                r = n % REP
                if r == 0:
                    pe.wait_ge(bank_b.free.sem, bank_b.free.at(here, B_USE[f"heads {u}"]))
                    pe.wait_ge(bank_s.free.sem, bank_s.free.at(here, S_USE[f"cmp probs {u}"] + 1))
                pe.wait_ge(bank_a.free.sem, bank_a.free.at(here, A_USE[f"probs {n}"] + 1))
                o = bank_b.tile[:, r * P:(r + 1) * P]
                nb = nk // P
                for b in range(2):
                    for kb in range(nb):
                        i = b * nb + kb
                        pe.matmul(o, val[:, kb, b, g * DH:(g + 1) * DH], pT[:, n % 2, i * P:(i + 1) * P],
                                  start=(i == 0), stop=False)
                mm = pe.matmul(o, vcmp[:, g, :], pcT[:, r * P:(r + 1) * P], start=False, stop=True)
                if r == REP - 1:
                    mm.then_inc(bank_b.full.sem, 1)

            def attention_side(t):
                if t not in STEP_PERIODS:
                    return
                m = STEP_PERIODS.index(t)
                if 1 <= m <= NSTEP:
                    probs_turn(m - 1)
                if 2 <= m:
                    head_out(m - 2)
                if m < NSTEP:
                    scores(m)

            def pooled(i):
                pe.wait_ge(bank_s.free.sem, bank_s.free.at(here, S_USE[f"pooled {i}"]))
                t = T_POOL[i // 2]
                loaded(t)
                for tok in range(TOKS):
                    b = chunk_bank(C_U + i // 2, tok)
                    pe.wait_ge(chunk_free[b].sem, chunk_free[b].at(here, (C_U + i // 2) // 2 + 1))
                m = raw[t % 4][:, (i % 2) * 384:(i % 2 + 1) * 384]
                for k in range(2):
                    for tok in range(TOKS):
                        lhs = uc[:, tok * 512 + (i % 2) * PG + k * P:tok * 512 + (i % 2) * PG + (k + 1) * P]
                        o = k * T + tok * P
                        mm = pe.matmul(bank_s.tile[:, o:(k + 1) * T], lhs,
                                       m[:, 0:T] if tok == 0 else m[:, T:T + P],
                                       start=(tok == 0), stop=(tok == 1))
                mm.then_inc(bank_s.full.sem, 1)

            def mix(i):
                pe.wait_ge(bank_a.free.sem, bank_a.free.at(here, A_USE[f"mix {i}"]))
                pe.wait_ge(bank_s.free.sem, bank_s.free.at(here, S_USE[f"pooled {i}"] + 1))
                w = raw[T_POOL[i // 2] % 4][:, 768:1792].rearrange("p (g k c) -> p g k c", g=2, k=2)
                for d in range(2):
                    for k in range(2):
                        mm = pe.matmul(bank_a.tile[:, d * T:(d + 1) * T], w[:, i % 2, k, d * P:(d + 1) * P],
                                       pooledT[:, k, :], start=(k == 0), stop=(k == 1))
                mm.then_inc(bank_a.full.sem, 1)

            def columns(unit):
                pe.wait_ge(acc_step.sem, unit.at(here, 16, 4 + 16))
                pe.wait_ge(mod_free.sem, unit.at(here, 2, 1))
                for k in range(8):
                    mm = pe.matmul(mod_ps[:, k:k + 1], acc[:, k * P:(k + 1) * P], ones[:, 0:1],
                                   start=True, stop=True)
                mm.then_inc(acc_summed.sem, 2)

            def spread(unit, half):
                if half == 0:
                    pe.wait_ge(acc_step.sem, unit.at(here, 16, 4 + 16))
                pe.wait_ge(mod_free.sem, unit.at(here, 2, 1 + half))
                pe.matmul(mod_ps[:], ones, acc[:, half * 512:(half + 1) * 512], start=True,
                          stop=True).then_inc(acc_summed.sem, 1)

            def reduce_at(t):
                for i in range(2):
                    if t in ADA_REDUCE[i]:
                        spread(GATE1[i], ADA_REDUCE[i].index(t))
                for i in range(4):
                    if t in ADA_REDUCE[2 + i]:
                        with pe.If(here.layer < 1):
                            columns(FIRST_MOD2[i])

            def middle(t):
                if t == 19:
                    cmp_out()
                if t == 24:
                    cmp_scores(0)
                if t == 28:
                    stage_turn(bank_a, A_USE["q 1"], ST_Q + 2, 0, 4)
                    stage_turn(bank_s, S_USE["q 1"], ST_Q + 3, 1, 4)
                if t == 29:
                    cmp_scores(1)
                for u in range(4):
                    if t == STEP_PERIODS[4 * u + 1]:
                        cmp_probs_turn(u)
                for i in range(4):
                    if t == MIX_AT[i]:
                        mix(i)
                for i in range(4):
                    if t == POOLED_AT[i]:
                        pooled(i)
                reduce_at(t)

            def mlp_part(o, ups, groups, sums):
                t0, c0 = T_MLP + o * PART_TILES, C_MLP + o * PART_CHUNKS

                def use(k):
                    return (A_MLP, B_MLP)[k % 2] + 3 * o + k // 2

                def bank_of(k):
                    return bank_a if k % 2 == 0 else bank_b

                def turn(k):
                    pe.wait_ge(bank_of(k).free.sem, bank_of(k).free.at(here, use(k)))
                    for tok in range(TOKS):
                        b = chunk_bank(c0 + k, tok)
                        pe.wait_ge(chunk_free[b].sem, chunk_free[b].at(here, (c0 + k) // 2 + 1))
                    for i in range(2):
                        for tok in range(TOKS):
                            at = (i * TOKS + tok) * P
                            src = tok * 256 + i * P
                            mm = pe.transpose(bank_of(k).tile[:, at:at + P], bufb[:, k % 2, src:src + P], ident)
                    mm.then_inc(bank_of(k).full.sem, 1)

                def middle(m):
                    for k in turned_at(o, ups, m):
                        turn(k)
                    sums(m)

                if o == 0:
                    norm(2, t0, c0)
                for m in range(8 if o == 0 else 0, 4 * ups):
                    tile(t0 + m, c0 + m // 4, h_rows(m % 4), m % 4 == 0, m % 4 == 3, lambda m=m: middle(m))
                for m in range(4 * ups, 4 * (ups + groups)):
                    n, g = divmod(m - 4 * ups, groups)
                    if n == 0:
                        for k in (2 * g, 2 * g + 1):
                            pe.wait_ge(bank_of(k).free.sem, bank_of(k).free.at(here, use(k) + 1))
                    tile(t0 + m, c0 + ups + n, a_rows(g), g == 0, g == groups - 1, lambda m=m: middle(m))

            def gate2_sums(m):
                for unit, at in zip(GATE2, GATE2_REDUCE):
                    if m in at:
                        spread(unit, at.index(m))

            def next_sums(units, reductions):
                def sums(m):
                    for unit, at in zip(units, reductions):
                        if m in at:
                            with pe.If(here.layer < DEPTH - 1):
                                columns(unit)
                return sums

            pe.sem_inc(gemm_done.sem, 8)
            for b in range(4):
                pe.sem_inc(chunk_free[b].sem, 1)
            for bank in (bank_s, bank_a, bank_b):
                pe.sem_inc(bank.free.sem, 1)
            pe.sem_inc(mod_free.sem, 1)
            pe.wait_ge(first_landed.sem, 32)
            for q in range(FIRST_UNITS):
                columns(Unit(q))

            with pe.Fori(0, DEPTH) as layer:
                here.layer = layer
                norm(1, T_KV, C_KV)
                for t in range(8, 12):
                    if t == 8:
                        for tok, (bank, uses) in enumerate(((bank_a, A_USE), (bank_b, B_USE))):
                            b = chunk_bank(C_KV, tok)
                            pe.wait_ge(chunk_free[b].sem, chunk_free[b].at(here, C_KV // 2 + 1))
                            stage_turn(bank, uses["kv 0"], None, tok, 4, qT[:, tok].rearrange("p h t -> p (h t)"))
                    if t == 10:
                        stage_turn(bank_a, A_USE["kv 1"], ST_KV, 0, 2)
                        stage_turn(bank_b, B_USE["kv 1"], ST_KV + 1, 1, 2)
                    tile(t, C_KV + 2, h_rows(t % 4), t == 8, t == 11, lambda t=t: middle(t))
                gate_logits()
                hidden(0)
                reduce_at(12)
                gates_turn()
                stage_turn(bank_a, A_USE["kv 2"], ST_KV + 2, 0, 2)
                stage_turn(bank_b, B_USE["kv 2"], ST_KV + 3, 1, 2)
                reduce_at(13)
                hidden(1)
                reduce_at(14)
                for t in range(18, 26):
                    if t == 19:
                        hidden_turn()
                    if t == 22:
                        kcmp_turn()
                    if t == 24:
                        stage_turn(bank_a, A_USE["q 0"], ST_Q, 0, 4)
                        stage_turn(bank_b, B_USE["q 0"], ST_Q + 1, 1, 4)
                    attention_side(t)
                    g = (t - 18) % 4
                    tile(t, C_Q + (t - 18) // 4, h_rows(g), g == 0, g == 3, lambda t=t: middle(t))
                for i, t in enumerate((*range(T_U0, T_U0 + 4), *T_U1)):
                    attention_side(t)
                    g = i % 4
                    tile(t, C_U + i // 4, h_rows(g), g == 0, g == 3, lambda t=t: middle(t))
                for n, tiles in enumerate(T_PASS1):
                    for i, t in enumerate(tiles):
                        attention_side(t)
                        if n == 0 and i == 0:
                            for j in (0, 1):
                                pe.wait_ge(bank_a.free.sem, bank_a.free.at(here, A_USE[f"mix {j}"] + 1))
                        if n == 0 and i == 1:
                            for u in (0, 1):
                                pe.wait_ge(bank_b.free.sem, bank_b.free.at(here, B_USE[f"heads {u}"] + 1))
                        tile(t, C_PASS1 + n, a_rows(2 * i), i == 0, i == 1, lambda t=t: middle(t))
                for n in range(4):
                    for i in range(2):
                        t = T_PASS2 + 2 * n + i
                        attention_side(t)
                        if n == 0 and i == 0:
                            for j in (2, 3):
                                pe.wait_ge(bank_a.free.sem, bank_a.free.at(here, A_USE[f"mix {j}"] + 1))
                        if n == 0 and i == 1:
                            for u in (2, 3):
                                pe.wait_ge(bank_b.free.sem, bank_b.free.at(here, B_USE[f"heads {u}"] + 1))
                        rows = a_rows(1) if i == 0 else h_rows(0)
                        tile(t, C_PASS2 + n, rows, i == 0, i == 1, lambda t=t: middle(t))
                mlp_part(0, PART_UP, PART_G, gate2_sums)
                with pe.Fori(0, PARTS - 1) as part:
                    here.part = part
                    mlp_part(1, PART_UP, PART_G, next_sums(NEXT_LOOP, LOOP_REDUCE))
                here.part = None
                mlp_part(PARTS, LAST_UP, LAST_G, next_sums(NEXT_LAST, LAST_REDUCE))

        @block.scalar
        def _(act):
            here = Place()

            def split_hi(t, a):
                h = half_of(t) + a
                if a == 0:
                    act.wait_ge(raw_landed[t % 4].sem, raw_landed[t % 4].at(here, 16 * (t // 4 + 1)))
                act.wait_ge(gemm_done.sem, gemm_done.at(here, 2 * h - 6))
                act.activation(whi[h % 4][:].rearrange("p k c -> p (k c)"),
                               raw[t % 4][:, a * 1024:(a + 1) * 1024], ACT.Copy).then_inc(hi_ready.sem, 1)

            def chunk_done(t, tok):
                act.wait_ge(gemm_done.sem, gemm_done.at(here, 2 * half_of(t) + 2 + tok + 1))

            def square_heads(c, tok, n, scratch):
                for i in range(n):
                    o = (tok * n + i) * DH
                    act.activation(scratch[:, o:o + DH], ps[chunk_bank(c, tok)][:, i * DH:(i + 1) * DH],
                                   ACT.Square, accum_out=ss[:, tok, i:i + 1])

            def copy_chunk(t, c, dst, heads=0):
                for tok in range(TOKS):
                    chunk_done(t, tok)
                    if heads:
                        square_heads(c, tok, heads, uc[:])
                    act.activation(dst(tok), ps[chunk_bank(c, tok)][:], ACT.Copy)\
                        .then_inc(chunk_free[chunk_bank(c, tok)].sem, 1)

            def copy_keys(t, c, branch):
                for tok in range(TOKS):
                    chunk_done(t, tok)
                    bank = ps[chunk_bank(c, tok)]
                    square_heads(c, tok, KV, pooledT[:].rearrange("p k t -> p (k t)"))
                    act.activation(bufb[:, tok, 0:256], bank[:, 0:256], ACT.Copy)
                    act.activation(val[:, tok, branch, :], bank[:, 256:512], ACT.Copy)\
                        .then_inc(chunk_free[chunk_bank(c, tok)].sem, 1)

            def take(bank, use, dst, src, scale=1.0):
                act.wait_ge(bank.full.sem, bank.full.at(here, use + 1))
                act.activation(dst, src, ACT.Copy, scale=scale).then_inc(bank.free.sem, 1)

            def norm(which, t0):
                split_hi(t0 + 1, 0)
                split_hi(t0 + 1, 1)
                bank_uses = ((bank_a, A_USE), (bank_b, B_USE))
                for j in range(8):
                    bank, uses = bank_uses[j % 2]
                    act.wait_ge(bank.free.sem, bank.free.at(here, uses[f"norm{which} {j}"] + 1))
                    act.activation(h_hi[:, 2 * j:2 * j + 2, :].rearrange("p k t -> p (k t)"), bufa[:, j % 2, :],
                                   ACT.Copy).then_inc(norm_hi.sem, 1)
                    if j >= 2:
                        split_hi(t0 + j, 0)
                        split_hi(t0 + j, 1)

            def square(i, n, tok, updated):
                if updated is not None:
                    act.wait_ge(x_updated.sem, x_updated.at(here, updated))
                act.wait_ge(squared.sem, squared.at(here, i - 1))
                act.activation(h_hi[:, 8 + 2 * tok:10 + 2 * tok, :].rearrange("p k t -> p (k t)"),
                               x[:, tok, n * 512:(n + 1) * 512], ACT.Square,
                               accum_out=ssq[:, tok, n:n + 1]).then_inc(squared.sem, 1)

            def exp(n):
                u, g, q, h, nk = step_of(n)
                act.wait_ge(biased.sem, biased.at(here, n + 1))
                for b in range(2):
                    row = bufa[:, n % 2, b * nk:(b + 1) * nk]
                    last = act.activation(row, row, ACT.Exp, bias=nmax[:, n % 2, b:b + 1],
                                          accum_out=sums[:, n % 2, b:b + 1])
                last.then_inc(exped.sem, 1)

            def cmp_exp(g):
                act.wait_ge(cmp_biased.sem, cmp_biased.at(here, g + 1))
                row = pc[:, g].rearrange("p n c -> p (n c)")
                act.activation(row, row, ACT.Exp).then_inc(cmp_exped.sem, 1)

            def heads_to_rows(u):
                g, q = u // TOKS, u % TOKS
                act.wait_ge(bank_b.full.sem, bank_b.full.at(here, B_USE[f"heads {u}"] + 1))
                dst = a_hi[:, 8:12, q * P:(q + 1) * P] if g == 0 else h_hi[:, 0:4, q * P:(q + 1) * P]
                act.activation(dst, bank_b.tile[:].rearrange("p (r t) -> p r t", r=REP), ACT.Copy)\
                    .then_inc(heads_hi.sem, 1)

            def mixed(i):
                act.wait_ge(bank_a.full.sem, bank_a.full.at(here, A_USE[f"mix {i}"] + 1))
                if i % 2 == 1:
                    act.sem_inc(raw_free[T_POOL[i // 2] % 4].sem, 1)
                for d in range(2):
                    k = 2 * i + d
                    last = act.activation(a_hi[:, k, :], bank_a.tile[:, d * T:(d + 1) * T], ACT.Copy,
                                          scale=cv[:, CV["pool_scale"] + k:CV["pool_scale"] + k + 1])
                last.then_inc(mix_hi.sem, 1)

            def period(t, nxt):
                m = STEP_PERIODS.index(t) if t in STEP_PERIODS else -1
                if t == 7:
                    copy_chunk(6, C_KV, lambda tok: qT[:, tok, 0:4, :].rearrange("p h t -> p (h t)"))
                if t == 8:
                    copy_keys(7, C_KV + 1, 0)
                if t == 8:
                    for tok, (bank, uses) in enumerate(((bank_a, A_USE), (bank_b, B_USE))):
                        take(bank, uses["kv 0"],
                             uc[:].rearrange("p (n t) -> p n t", n=4)[:, :, tok * P:(tok + 1) * P],
                             bank.tile[:].rearrange("p (n t) -> p n t", n=4))
                if t == 10:
                    act.wait_ge(cv_landed.sem, cv_landed.at(here, 16))
                    take_keys(0)
                if t == 19:
                    take(bank_s, S_USE["hidden turned"], hid[:],
                         bank_s.tile[:, 0:2 * P].rearrange("p (i n) -> p i n", i=2)[:, :, 0:KV * NC])
                if t == 22:
                    take(bank_a, A_USE["kcmp"], kcT[:, :, 0:NC],
                         bank_a.tile[:, 0:KV * P].rearrange("p (g c) -> p g c", g=KV)[:, :, 0:NC],
                         cv[:, CV["k_gain"]:CV["k_gain"] + 1])
                if t == 22:
                    copy_chunk(21, C_Q, lambda tok: bufb[:, tok, :], REP)
                if t == 24:
                    take_queries(0, ((bank_a, A_USE), (bank_b, B_USE)))
                if t == 26:
                    copy_chunk(25, C_Q + 1, lambda tok: bufb[:, tok, :], REP)
                if 1 <= m <= NSTEP:
                    n = m - 1
                    nk = step_of(n)[4]
                    take(bank_a, A_USE[f"probs {n}"], pT[:, n % 2, 0:2 * nk], bank_a.tile[:, 0:2 * nk])
                if t == 30:
                    copy_chunk(29, C_U, lambda tok: uc[:, tok * 512:(tok + 1) * 512])
                if t == 35:
                    copy_chunk(34, C_U + 1, lambda tok: uc[:, tok * 512:(tok + 1) * 512])
                for u in range(4):
                    if t == STEP_PERIODS[4 * u + 5]:
                        heads_to_rows(u)
                if nxt is not None:
                    split_hi(nxt, 0)
                if 0 <= m < NSTEP:
                    exp(m)
                if nxt is not None:
                    split_hi(nxt, 1)
                if t == 11:
                    act.wait_ge(raw_landed[T_GL % 4].sem, raw_landed[T_GL % 4].at(here, 16 * (T_GL // 4 + 1)))
                    act.activation(gate_w[0], raw[T_GL % 4][:, 0:24 * KT], ACT.Copy).then_inc(gl_hi.sem, 1)
                if t == 24:
                    cmp_exp(0)
                if t == 28:
                    take_queries(1, ((bank_a, A_USE), (bank_s, S_USE)))
                if t == 29:
                    cmp_exp(1)
                for u in range(4):
                    if t == STEP_PERIODS[4 * u + 1]:
                        take(bank_s, S_USE[f"cmp probs {u}"], pcT[:], bank_s.tile[0:NC, :])
                for i in range(4):
                    if t == MIX_AT[i]:
                        mixed(i)
                for i in range(4):
                    if t == POOLED_AT[i]:
                        take(bank_s, S_USE[f"pooled {i}"], pooledT[:].rearrange("p k t -> p (k t)"),
                             bank_s.tile[:])
                if t in (46, 48, 50):
                    n = (t - 46) // 2
                    for tok in range(TOKS):
                        square(2 * n + tok, n, tok, 8 + 2 * n + tok + 1)

            def take_keys(branch):
                for tok, (bank, uses) in enumerate(((bank_a, A_USE), (bank_b, B_USE))):
                    take(bank, uses[f"kv {branch + 1}"], kT[:, branch, :, tok * P:(tok + 1) * P],
                         bank.tile[:, 0:256].rearrange("p (g t) -> p g t", g=KV),
                         cv[:, CV["k_gain"] + 1 + branch:CV["k_gain"] + 2 + branch])

            def take_queries(g, banks):
                for tok, (bank, uses) in enumerate(banks):
                    take(bank, uses[f"q {g}"], qT[:, tok, REP * g:REP * (g + 1), :],
                         bank.tile[:].rearrange("p (r t) -> p r t", r=REP), qgs[:, 0:1])

            def direct():
                copy_keys(11, C_KV + 2, 1)
                act.wait_ge(gl_done.sem, gl_done.at(here, 1))
                b = chunk_bank(C_GL, 0)
                act.activation(uc[0:24, 2 * P:4 * P], ps[b][0:24, 0:T], ACT.Exp, scale=-1.0)\
                    .then_inc(chunk_free[b].sem, 1)
                take_keys(1)
                split_hi(T_Q, 0)
                split_hi(T_Q, 1)
                act.wait_ge(bank_s.full.sem, bank_s.full.at(here, S_USE["hidden"] + 1))
                act.sem_inc(raw_free[(T_CMP1 + 3) % 4].sem, 1)
                act.activation(uc[0:KV * NC, 0:2 * P], bank_s.tile[0:KV * NC, 0:2 * P], ACT.Exp, scale=-1.0)\
                    .then_inc(hid_exp.sem, 1)

            def mlp_part(o, ups, groups, last):
                t0, c0 = T_MLP + o * PART_TILES, C_MLP + o * PART_CHUNKS
                tiles = 4 * (ups + groups)

                def silu(k):
                    if k == 0 and o > 0:
                        act.wait_ge(x_updated.sem, x_updated.at(here, 16 + 8 * o))
                    for tok in range(TOKS):
                        if k >= 2:
                            b = chunk_bank(c0 + k, tok)
                            act.wait_ge(chunk_free[b].sem, chunk_free[b].at(here, (c0 + k - 2) // 2 + 1))
                        chunk_done(t0 + (6 if o == 0 and k == 0 else 4 * k + 3), tok)
                        act.activation(bufa[:, k % 2, tok * 256:(tok + 1) * 256],
                                       ps[chunk_bank(c0 + k, tok)][:, 0:256], ACT.Silu)\
                            .then_inc(silu_done.sem, 1)

                def rows(k):
                    bank, base = (bank_a, A_MLP) if k % 2 == 0 else (bank_b, B_MLP)
                    act.wait_ge(bank.full.sem, bank.full.at(here, base + 3 * o + k // 2 + 1))
                    act.activation(a_hi[:, 2 * k:2 * k + 2, :].rearrange("p k t -> p (k t)"), bank.tile[:],
                                   ACT.Copy).then_inc(ff_hi.sem, 1)

                for m in range(7 if o == 0 else 0, tiles):
                    for k in done_before(o, ups, m):
                        silu(k)
                    n = (m - 4 * ups) // groups - 1
                    if last and m >= 4 * ups and (m - 4 * ups) % groups == 0 and 0 <= n:
                        for tok in range(TOKS):
                            square(8 + 2 * n + tok, n, tok, 16 + 8 * o + 2 * n + tok + 1)
                    if not (last and m == tiles - 1):
                        split_hi(t0 + m + 1, 0)
                        split_hi(t0 + m + 1, 1)
                    for k in turned_at(o, ups, m):
                        rows(k)
                if last:
                    with act.If(here.layer < DEPTH - 1):
                        split_hi(TILES, 0)
                        split_hi(TILES, 1)
                    for tok in range(TOKS):
                        square(14 + tok, 3, tok, 16 + 8 * o + 6 + tok + 1)

            act.dma_start(ccol[:], c_col).then_inc(cond_ready.sem, 16)
            act.wait_ge(cond_ready.sem, 16)
            act.activation(cond[:], ccol[:], ACT.Silu).then_inc(cond_ready.sem, 1)
            act.wait_ge(x_landed.sem, 16)
            for n in range(4):
                for tok in range(TOKS):
                    i = 2 * n + tok
                    if i >= 2:
                        act.wait_ge(squared.sem, i - 1)
                    act.activation(h_hi[:, 8 + 2 * tok:10 + 2 * tok, :].rearrange("p k t -> p (k t)"),
                                   x[:, tok, n * 512:(n + 1) * 512], ACT.Square,
                                   accum_out=ssq[:, tok, n:n + 1]).then_inc(squared.sem, 1)

            split_hi(0, 0)
            split_hi(0, 1)

            with act.Fori(0, DEPTH) as layer:
                here.layer = layer
                norm(1, 0)
                act.dma_start(cv[:], vec[bass.ds(layer, 1)].rearrange("o p c -> (o p) c"))\
                    .then_inc(cv_landed.sem, 16)
                act.dma_start(gate[:], b_ada[bass.ds(layer, 1), 2 * D:3 * D].partition_broadcast(P))\
                    .then_inc(gate_landed.sem, 16)
                for t in range(7, 12):
                    period(t, t + 1 if t < 11 else None)
                direct()
                split_tiles = [t for t in range(T_Q, T_MLP) if t not in DIRECT]
                for t, nxt in zip(split_tiles, split_tiles[1:] + [T_MLP]):
                    period(t, nxt)
                for tok in range(TOKS):
                    square(6 + tok, 3, tok, 8 + 6 + tok + 1)
                norm(2, T_MLP)
                act.dma_start(nv[:], vec_next[bass.ds(layer + 1, 1)].rearrange("o p c -> (o p) c"))\
                    .then_inc(nv_landed.sem, 16)
                act.dma_start(gate[:], b_ada[bass.ds(layer, 1), 5 * D:6 * D].partition_broadcast(P))\
                    .then_inc(gate_landed.sem, 16)
                mlp_part(0, PART_UP, PART_G, False)
                with act.Fori(0, PARTS - 1) as part:
                    here.part = part
                    mlp_part(1, PART_UP, PART_G, False)
                here.part = None
                mlp_part(PARTS, LAST_UP, LAST_G, True)

        @block.vector
        def _(dve):
            here = Place()
            steps = [0]

            def step():
                steps[0] += 1
                return dve_step.at(here, steps[0])

            def split_lo(t, a):
                h = half_of(t) + a
                dve.wait_ge(hi_ready.sem, hi_ready.at(here, h + 1))
                dve.tensor_tensor(wlo[h % 4][:].rearrange("p k c -> p (k c)"),
                                  raw[t % 4][:, a * 1024:(a + 1) * 1024],
                                  whi[h % 4][:].rearrange("p k c -> p (k c)").bitcast(F32), ALU.subtract)\
                    .then_inc(lo_ready.sem, 1)

            def ada_sums(unit, at, t):
                first = sum(n for tt, n in at.items() if tt < t)
                for k in range(first, first + at.get(t, 0)):
                    dve.wait_ge(ada_landed[k % 4].sem, unit.at(here, 64, 16 * (k // 4 + 1)))
                    if k == 0:
                        if here.layer is not None or unit.first > 0:
                            dve.wait_ge(acc_summed.sem, unit.at(here, 2, 0))
                        dve.tensor_scalar(acc[:], ada[0][:], cond[:, 0:1], None, ALU.mult)\
                            .then_inc(acc_step.sem, 1)
                    else:
                        dve.wait_ge(acc_step.sem, unit.at(here, 16, 4 + k))
                        dve.scalar_tensor_tensor(acc[:], ada[k % 4][:], cond[:, k:k + 1], acc[:], ALU.mult,
                                                 ALU.add).then_inc(acc_step.sem, 1)

            def take_columns(unit, u):
                flat = mod[:].rearrange("p u a k -> p (u a k)")

                def cols(table, first):
                    return table[:, first:first + 8] if here.part is None else table[:, bass.ds(first, 8)]

                dve.wait_ge(acc_summed.sem, unit.at(here, 2, 2))
                dve.tensor_tensor(cols(flat, u * 16), mod_ps[:, 0:8], cols(nv, u * 8 + NV_BIAS), ALU.add)\
                    .then_inc(mod_free.sem, 2)
                dve.wait_ge(mod_free.sem, unit.at(here, 2, 3))
                dve.scalar_tensor_tensor(cols(flat, u * 16 + 8), cols(flat, u * 16), 1.0,
                                         cols(nv, u * 8 + NV_GAIN), ALU.add, ALU.mult)

            def take_spread(unit, i, half, biases):
                if i == 0 and half == 0:
                    dve.wait_ge(gate_landed.sem, gate_landed.at(here, 16 * biases))
                dve.wait_ge(acc_summed.sem, unit.at(here, 2, half + 1))
                g = gate[:, i * 1024 + half * 512:i * 1024 + (half + 1) * 512]
                dve.tensor_tensor(g, mod_ps[:], g, ALU.add).then_inc(mod_free.sem, 1)

            def rstd(v, width):
                y, e = root[0:v.shape[0]], root_err[0:v.shape[0]]
                if len(v.shape) == 3:
                    y, e = (r.rearrange("p (q n) -> p q n", q=TOKS)[:, :, 0:v.shape[2]] for r in (y, e))
                else:
                    y, e = y[:, 0:v.shape[1]], e[:, 0:v.shape[1]]
                dve.tensor_scalar(v, v, 1.0 / width, EPS, ALU.mult, ALU.add).then_inc(dve_step.sem, 1)
                dve.wait_ge(dve_step.sem, step())
                dve.tensor_scalar(y.bitcast(I32), v.bitcast(I32), -0.5, float(0x5f3759df), ALU.mult, ALU.add)\
                    .then_inc(dve_step.sem, 1)
                dve.wait_ge(dve_step.sem, step())
                for i in range(3):
                    dve.tensor_tensor(e, y, y, ALU.mult).then_inc(dve_step.sem, 1)
                    dve.wait_ge(dve_step.sem, step())
                    dve.scalar_tensor_tensor(e, e, -0.5, v, ALU.mult, ALU.mult).then_inc(dve_step.sem, 1)
                    dve.wait_ge(dve_step.sem, step())
                    dve.scalar_tensor_tensor(v if i == 2 else y, e, 1.5, y, ALU.add, ALU.mult)\
                        .then_inc(dve_step.sem, 1)
                    dve.wait_ge(dve_step.sem, step())

            def norm(which, t0):
                dve.wait_ge(squared.sem, squared.at(here, 0 if which == 1 else 8))
                dve.tensor_reduce(rs[:], ssq[:], X, ALU.add).then_inc(dve_step.sem, 1)
                dve.wait_ge(dve_step.sem, step())
                rstd(rs[:], D)
                uses = (A_USE, B_USE)
                banks = (bank_a, bank_b)

                def stage(j):
                    if j >= 2:
                        use = uses[j % 2][f"norm{which} {j - 2}"]
                        dve.wait_ge(banks[j % 2].full.sem, banks[j % 2].full.at(here, use + 1))
                    for tok in range(TOKS):
                        last = dve.tensor_scalar(bufb[:, j % 2, tok * 256:(tok + 1) * 256],
                                                 x[:, tok, j * 256:(j + 1) * 256], rs[:, tok:tok + 1], None,
                                                 ALU.mult)
                    last.then_inc(stage_ready.sem, 1)

                stage(0)
                stage(1)
                unit = 4 * (which - 1)
                for j in range(8):
                    bank, use = banks[j % 2], uses[j % 2][f"norm{which} {j}"]
                    dve.wait_ge(bank.full.sem, bank.full.at(here, use + 1))
                    for i in range(2):
                        u, k = divmod(2 * j + i, 8)
                        last = dve.tensor_scalar(bufa[:, j % 2, i * T:(i + 1) * T],
                                                 bank.tile[:, i * T:(i + 1) * T],
                                                 mod[:, unit + 2 + u, 1, k:k + 1],
                                                 mod[:, unit + u, 0, k:k + 1], ALU.mult, ALU.add)
                    last.then_inc(bank.free.sem, 1)
                    if j + 2 < 8:
                        stage(j + 2)
                    dve.wait_ge(norm_hi.sem, norm_hi.at(here, 8 * (which - 1) + j + 1))
                    dve.tensor_tensor(h_lo[:, 2 * j:2 * j + 2, :].rearrange("p k t -> p (k t)"),
                                      bufa[:, j % 2, :],
                                      h_hi[:, 2 * j:2 * j + 2, :].rearrange("p k t -> p (k t)").bitcast(F32),
                                      ALU.subtract).then_inc(h_ready.sem, 1)
                    if j != 1:
                        split_lo(t0 + max(j, 1), 0)
                        split_lo(t0 + max(j, 1), 1)

            def head_sums(tok, rows, n, scratch):
                dve.tensor_tensor(scratch, rows, rows, ALU.mult).then_inc(dve_step.sem, 1)
                dve.wait_ge(dve_step.sem, step())
                dve.tensor_reduce(ss[0:rows.shape[0], tok, 0:n], scratch.rearrange("p (n d) -> p n d", n=n),
                                  X, ALU.add).then_inc(dve_step.sem, 1)
                dve.wait_ge(dve_step.sem, step())

            def scale_heads(tok, rows, n):
                heads = rows.rearrange("p (n d) -> p n d", n=n)
                part = rows.shape[0]
                dve.tensor_tensor(heads, heads, ss[0:part, tok, 0:n].unsqueeze(2).to_broadcast([part, n, DH]),
                                  ALU.mult).then_inc(stage_ready.sem, 1)

            def stage_rstd(c, n):
                for tok in range(TOKS):
                    b = chunk_bank(c, tok)
                    dve.wait_ge(chunk_free[b].sem, chunk_free[b].at(here, c // 2 + 1))
                rstd(ss[:, :, 0:n], DH)

            def stage_scale(n):
                for tok in range(TOKS):
                    scale_heads(tok, bufb[:, tok, 0:n * DH], n)

            def blocks(i):
                if i == 0:
                    dve.wait_ge(bank_a.free.sem, bank_a.free.at(here, A_USE["kv 0"] + 1))
                    dve.wait_ge(bank_b.free.sem, bank_b.free.at(here, B_USE["kv 0"] + 1))
                src = uc[:, i * 512:(i + 1) * 512].rearrange("p (g c s) -> p g c s", g=KV, s=CMP_STRIDE)
                dst = (bufa, pT)[i][:].rearrange("p a b -> p (a b)")[:, 0:KV * NC * CMP_LEN]\
                    .rearrange("p (g c s) -> p g c s", g=KV, s=CMP_LEN)
                for a in range(2):
                    o = CV["pe"] + i * CMP_LEN + a * CMP_STRIDE
                    pe_cols = cv[:, o:o + CMP_STRIDE].unsqueeze(1).to_broadcast([P, NC, CMP_STRIDE])
                    for g in range(KV):
                        last = dve.tensor_tensor(dst[:, g, :, a * CMP_STRIDE:(a + 1) * CMP_STRIDE],
                                                 src[:, g, a:a + NC, :], pe_cols, ALU.add)
                last.then_inc(blocks_ready.sem, 1)

            def sigmoid_gates():
                dve.wait_ge(gl_turned.sem, gl_turned.at(here, 1))
                b = chunk_bank(C_GL, 1)
                rows = gates[:].rearrange("p q h b -> p q (h b)")
                dve.tensor_scalar(rows, ps[b][:, 0:T].rearrange("p (q t) -> p q t", q=TOKS)[:, :, 0:24], 1.0, None,
                                  ALU.add).then_inc(chunk_free[b].sem, 1)
                dve.wait_ge(chunk_free[b].sem, chunk_free[b].at(here, C_GL // 2 + 1))
                dve.reciprocal(rows, rows).then_inc(dve_step.sem, 1)
                dve.wait_ge(dve_step.sem, step())

            def silu_hidden():
                rows = uc[0:KV * NC, 0:2 * P]
                dve.wait_ge(hid_exp.sem, hid_exp.at(here, 1))
                dve.tensor_scalar(rows, rows, 1.0, None, ALU.add).then_inc(dve_step.sem, 1)
                dve.wait_ge(dve_step.sem, step())
                dve.reciprocal(rows, rows).then_inc(dve_step.sem, 1)
                dve.wait_ge(dve_step.sem, step())
                dve.tensor_tensor(bufa[0:KV * NC, 0, 0:2 * P], bank_s.tile[0:KV * NC, 0:2 * P], rows, ALU.mult)\
                    .then_inc(bank_s.free.sem, 1)

            def take_cmp():
                use = S_USE["cmp out"]
                dve.wait_ge(bank_s.full.sem, bank_s.full.at(here, use + 1))
                dve.sem_inc(raw_free[T_CMP2 % 4].sem, 1)
                dve.tensor_copy(vcmp[:].rearrange("p g d -> p (g d)"), bank_s.tile[0:NC, 256:512])
                dve.tensor_copy(bufa[0:NC, 0, 0:256], bank_s.tile[0:NC, 0:256]).then_inc(bank_s.free.sem, 1)
                dve.wait_ge(bank_s.free.sem, bank_s.free.at(here, use + 1))
                head_sums(0, bufa[0:NC, 0, 0:256], KV, pooledT[0:NC, 0, :])
                rstd(ss[0:NC, 0, 0:KV], DH)
                scale_heads(0, bufa[0:NC, 0, 0:256], KV)

            def cmp_bias(g):
                use = S_USE[f"cmp scores {g}"]
                n = TOKS * REP * NC
                row = pc[:, g].rearrange("p n c -> p (n c)")
                dve.wait_ge(bank_s.full.sem, bank_s.full.at(here, use + 1))
                dve.tensor_tensor(row, bank_s.tile[:, 0:n], k_sb[:, K_CMP + g * n:K_CMP + (g + 1) * n], ALU.add)\
                    .then_inc(bank_s.free.sem, 1)
                dve.wait_ge(bank_s.free.sem, bank_s.free.at(here, use + 1))
                dve.tensor_reduce(m8[:], pc[:, g], X, ALU.max, negate=True).then_inc(dve_step.sem, 1)
                dve.wait_ge(dve_step.sem, step())
                dve.tensor_tensor(pc[:, g], pc[:, g], m8[:].unsqueeze(2).to_broadcast([P, 8, NC]), ALU.add)\
                    .then_inc(cmp_biased.sem, 1)

            def cmp_scale(g):
                dve.wait_ge(cmp_exped.sem, cmp_exped.at(here, g + 1))
                dve.tensor_reduce(f8[:], pc[:, g], X, ALU.add).then_inc(dve_step.sem, 1)
                dve.wait_ge(dve_step.sem, step())
                dve.reciprocal(f8[:], f8[:]).then_inc(dve_step.sem, 1)
                dve.wait_ge(dve_step.sem, step())
                f8v = f8[:].rearrange("p (q r) -> p q r", q=TOKS)
                dve.tensor_tensor(f8v, f8v, gates[:, :, REP * g:REP * (g + 1), 0], ALU.mult)\
                    .then_inc(dve_step.sem, 1)
                dve.wait_ge(dve_step.sem, step())
                dve.tensor_scalar(f8[:, 0:REP], f8[:, 0:REP], k_sb[:, K_SEEN:K_SEEN + 1], None, ALU.mult)\
                    .then_inc(dve_step.sem, 1)
                dve.wait_ge(dve_step.sem, step())
                dve.tensor_tensor(pc[:, g], pc[:, g], f8[:].unsqueeze(2).to_broadcast([P, 8, NC]), ALU.mult)\
                    .then_inc(cmp_ready.sem, 1)

            def bias(n):
                u, g, q, h, nk = step_of(n)
                use = S_USE[f"scores {n}"]
                if n >= 2:
                    dve.wait_ge(bank_a.full.sem, bank_a.full.at(here, A_USE[f"probs {n - 2}"] + 1))
                dve.wait_ge(bank_s.full.sem, bank_s.full.at(here, use + 1))
                rows = bufa[:, n % 2, 0:2 * nk].rearrange("p (b k) -> p b k", b=2)
                dist = k_sb[:, K_DIST + 2 * P - nk:K_DIST + 2 * P].unsqueeze(1).to_broadcast([P, 2, nk])
                dve.scalar_tensor_tensor(rows, dist, 2.0 ** -(h + 1),
                                         bank_s.tile[:, 0:2 * nk].rearrange("p (b k) -> p b k", b=2),
                                         ALU.mult, ALU.add).then_inc(bank_s.free.sem, 1)
                dve.wait_ge(bank_s.free.sem, bank_s.free.at(here, use + 1))
                dve.tensor_reduce(nmax[:, n % 2, :], rows, X, ALU.max, negate=True).then_inc(biased.sem, 1)

            def scale(n):
                u, g, q, h, nk = step_of(n)
                dve.wait_ge(exped.sem, exped.at(here, n + 1))
                dve.reciprocal(fac[:], sums[:, n % 2, :]).then_inc(dve_step.sem, 1)
                dve.wait_ge(dve_step.sem, step())
                dve.tensor_tensor(fac[:], fac[:], gates[:, q, h, 1:3], ALU.mult).then_inc(dve_step.sem, 1)
                dve.wait_ge(dve_step.sem, step())
                for b in range(2):
                    row = bufa[:, n % 2, b * nk:(b + 1) * nk]
                    last = dve.tensor_scalar(row, row, fac[:, b:b + 1], None, ALU.mult)
                last.then_inc(p_ready.sem, 1)

            def heads_to_rows(u):
                g, q = u // TOKS, u % TOKS
                dve.wait_ge(heads_hi.sem, heads_hi.at(here, u + 1))
                hi, lo = ((a_hi, a_lo), (h_hi, h_lo))[g]
                r0 = 8 if g == 0 else 0
                dve.tensor_tensor(lo[:, r0:r0 + 4, q * P:(q + 1) * P],
                                  bank_b.tile[:].rearrange("p (r t) -> p r t", r=REP),
                                  hi[:, r0:r0 + 4, q * P:(q + 1) * P].bitcast(F32), ALU.subtract)\
                    .then_inc(bank_b.free.sem, 1)

            def mixed(i):
                dve.wait_ge(mix_hi.sem, mix_hi.at(here, i + 1))
                for d in range(2):
                    k = 2 * i + d
                    last = dve.scalar_tensor_tensor(
                        a_lo[:, k, :], bank_a.tile[:, d * T:(d + 1) * T],
                        cv[:, CV["pool_scale"] + k:CV["pool_scale"] + k + 1],
                        a_hi[:, k, :].bitcast(F32), ALU.mult, ALU.subtract)
                last.then_inc(bank_a.free.sem, 1)

            def into_x(m, t, c, n, buf):
                for tok in range(TOKS):
                    b = chunk_bank(c, tok)
                    dve.wait_ge(gemm_done.sem, gemm_done.at(here, 2 * half_of(t) + 2 + tok + 1))
                    if m > 0:
                        dve.wait_ge(x_updated.sem, x_updated.at(here, 2 * m - 1 + tok))
                    dve.tensor_tensor(buf[:, tok, :], ps[b][:], gate[:, n * 512:(n + 1) * 512], ALU.mult)\
                        .then_inc(chunk_free[b].sem, 1)
                for tok in range(TOKS):
                    b = chunk_bank(c, tok)
                    dve.wait_ge(chunk_free[b].sem, chunk_free[b].at(here, c // 2 + 1))
                    xs = x[:, tok, n * 512:(n + 1) * 512]
                    dve.tensor_tensor(xs, xs, buf[:, tok, :], ALU.add).then_inc(x_updated.sem, 1)

            def conditioning(t):
                for i in range(2):
                    if t in ADA_REDUCE[i]:
                        take_spread(GATE1[i], i, ADA_REDUCE[i].index(t), 1)
                    ada_sums(GATE1[i], ADA_SUMS[i], t)
                if any(t in at for at in ADA_REDUCE[2:] + ADA_SUMS[2:]):
                    with dve.If(here.layer < 1):
                        for i in range(4):
                            if t in ADA_REDUCE[2 + i]:
                                take_columns(FIRST_MOD2[i], 4 + i)
                            ada_sums(FIRST_MOD2[i], ADA_SUMS[2 + i], t)

            def period(t, nxt):
                m = STEP_PERIODS.index(t) if t in STEP_PERIODS else -1
                if 0 <= m < NSTEP:
                    bias(m)
                for u in range(4):
                    if t == STEP_PERIODS[4 * u + 5]:
                        heads_to_rows(u)
                if nxt is not None:
                    split_lo(nxt, 0)
                if t == 7:
                    dve.wait_ge(cv_landed.sem, cv_landed.at(here, 16))
                    dve.tensor_scalar(qgs[:], cv[:, CV["q_gain"]:CV["q_gain"] + 1], DH ** -0.5, None, ALU.mult)
                if t == 25:
                    cmp_scale(0)
                if t == 30:
                    cmp_scale(1)
                if 0 <= m < NSTEP:
                    scale(m)
                if nxt is not None:
                    split_lo(nxt, 1)
                if t == 9:
                    blocks(0)
                if t == 10:
                    blocks(1)
                if t == 11:
                    dve.wait_ge(gl_hi.sem, gl_hi.at(here, 1))
                    dve.tensor_tensor(gate_w[1], raw[T_GL % 4][:, 0:24 * KT], gate_w[0].bitcast(F32), ALU.subtract)\
                        .then_inc(gl_lo.sem, 1)
                if t == 8:
                    stage_rstd(C_KV + 1, 2)
                    stage_scale(2)
                if t == 19:
                    take_cmp()
                if t == 22:
                    stage_rstd(C_Q, 4)
                    stage_scale(4)
                if t == 27:
                    stage_scale(4)
                if t == 24:
                    cmp_bias(0)
                if t == 29:
                    cmp_bias(1)
                for i in range(4):
                    if t == MIX_AT[i]:
                        mixed(i)
                for n in range(4):
                    if t == (38, 40, 42, 44)[n]:
                        into_x(n, T_PASS1[n][1], C_PASS1 + n, n, bufb)
                if t in (46, 48, 50):
                    n = (t - 46) // 2
                    into_x(4 + n, T_PASS2 + 2 * n + 1, C_PASS2 + n, n, bufb)
                conditioning(t)
                if t == 26:
                    stage_rstd(C_Q + 1, 4)

            def mlp_part(o, ups, groups, last, sums):
                t0, c0 = T_MLP + o * PART_TILES, C_MLP + o * PART_CHUNKS
                tiles = 4 * (ups + groups)

                def times_up(k):
                    if k >= 2:
                        bank, base = (bank_a, A_MLP) if k % 2 == 0 else (bank_b, B_MLP)
                        dve.wait_ge(bank.full.sem, bank.full.at(here, base + 3 * o + (k - 2) // 2 + 1))
                    for tok in range(TOKS):
                        dve.wait_ge(silu_done.sem, silu_done.at(here, 12 * o + 2 * k + tok + 1))
                        b = chunk_bank(c0 + k, tok)
                        dve.tensor_tensor(bufb[:, k % 2, tok * 256:(tok + 1) * 256],
                                          bufa[:, k % 2, tok * 256:(tok + 1) * 256], ps[b][:, 256:512],
                                          ALU.mult).then_inc(chunk_free[b].sem, 1)

                def rows(k):
                    bank = bank_a if k % 2 == 0 else bank_b
                    dve.wait_ge(ff_hi.sem, ff_hi.at(here, 6 * o + k + 1))
                    hi = a_hi[:, 2 * k:2 * k + 2, :].rearrange("p k t -> p (k t)").bitcast(F32)
                    dve.tensor_tensor(a_lo[:, 2 * k:2 * k + 2, :].rearrange("p k t -> p (k t)"), bank.tile[:],
                                      hi, ALU.subtract).then_inc(bank.free.sem, 1)

                def down(n):
                    into_x(8 + 4 * o + n, t0 + 4 * ups + groups * (n + 1) - 1, c0 + ups + n, n, bufa)

                for m in range(7 if o == 0 else 0, tiles):
                    for k in done_before(o, ups, m):
                        times_up(k)
                    n, g = divmod(m - 4 * ups, groups)
                    if m >= 4 * ups and g == 0 and n >= 1:
                        down(n - 1)
                    if not (last and m == tiles - 1):
                        split_lo(t0 + m + 1, 0)
                        split_lo(t0 + m + 1, 1)
                    for k in turned_at(o, ups, m):
                        rows(k)
                    sums(m)
                if last:
                    with dve.If(here.layer < DEPTH - 1):
                        split_lo(TILES, 0)
                        split_lo(TILES, 1)
                down(3)

            def gate2_sums(m):
                for i in range(2):
                    if m in GATE2_REDUCE[i]:
                        take_spread(GATE2[i], i, GATE2_REDUCE[i].index(m), 2)
                    ada_sums(GATE2[i], GATE2_SUMS[i], m)

            def next_sums(units, sums_at, reductions, first):
                def sums(m):
                    if not any(m in at for at in reductions + sums_at):
                        return
                    with dve.If(here.layer < DEPTH - 1):
                        for i, unit in enumerate(units):
                            if m in reductions[i]:
                                dve.wait_ge(nv_landed.sem, nv_landed.at(here, 16))
                                take_columns(unit, first + i if here.part is None else
                                             here.part * LOOP_UNITS + (first + i))
                            ada_sums(unit, sums_at[i], m)
                return sums

            dve.sem_inc(acc_step.sem, 4)
            dve.wait_ge(cond_ready.sem, 17)
            dve.wait_ge(first_landed.sem, 32)
            for q in range(FIRST_UNITS):
                ada_sums(Unit(q), {0: KT}, 0)
                take_columns(Unit(q), q)
            split_lo(0, 0)
            split_lo(0, 1)

            with dve.Fori(0, DEPTH) as layer:
                here.layer = layer
                norm(1, 0)
                for t in range(7, 12):
                    period(t, t + 1 if t < 11 else None)
                stage_rstd(C_KV + 2, 2)
                stage_scale(2)
                conditioning(12)
                sigmoid_gates()
                conditioning(13)
                split_lo(T_Q, 0)
                split_lo(T_Q, 1)
                silu_hidden()
                conditioning(14)
                split_tiles = [t for t in range(T_Q, T_MLP) if t not in DIRECT]
                for t, nxt in zip(split_tiles, split_tiles[1:] + [T_MLP]):
                    period(t, nxt)
                into_x(7, T_PASS2 + 7, C_PASS2 + 3, 3, bufb)
                norm(2, T_MLP)
                mlp_part(0, PART_UP, PART_G, False, gate2_sums)
                with dve.Fori(0, PARTS - 1) as part:
                    here.part = part
                    mlp_part(1, PART_UP, PART_G, False, next_sums(NEXT_LOOP, LOOP_SUMS, LOOP_REDUCE, 0))
                here.part = None
                mlp_part(PARTS, LAST_UP, LAST_G, True,
                         next_sums(NEXT_LAST, LAST_SUMS, LAST_REDUCE, LOOP_UNITS * (PARTS - 1)))
            assert steps[0] == DVE_STEPS, steps


def layer_stream(w_in, w_cmp1, w_cmp2, w_pool, w_out, w_gate_up, w_down, pool_m):
    out = np.zeros((TILES, P, 4 * COLS), np.float32)
    place = iter([t for t in range(TILES) if t not in DIRECT])

    def put(w, kts, cols):
        block = w.reshape(-1, P, w.shape[1])
        out[next(place)].reshape(P, 4, COLS)[:] = block[kts][:, :, cols].transpose(1, 0, 2)

    def chunk(w, first, kts):
        for g in range(0, len(kts), 4):
            put(w, kts[g:g + 4], np.arange(first, first + COLS))

    def in_turn(first_chunks):
        for g in range(4):
            for w, cols in first_chunks:
                put(w, every[4 * g:4 * g + 4], cols)

    every = list(range(KT))
    in_turn([(w_in, np.arange(f, f + COLS)) for f in (2048, 2560)])
    for first in (3072, 1024, 1536, 0, 512):
        chunk(w_in, first, every)
    out[T_GL][:, :384] = w_in[:, 3584:].reshape(KT, P, 24).transpose(1, 0, 2).reshape(P, 384)
    for i in range(2):
        w = w_cmp1[i].reshape(2, 16, P, P).transpose(0, 2, 1, 3)
        for a in range(2):
            out[T_CMP1 + 2 * i + a] = w[a].reshape(P, 16 * P)
    out[T_CMP2][:, :256] = w_cmp2.transpose(1, 0, 2).reshape(P, 256)
    for i, t in enumerate(T_POOL):
        out[t][:, :768] = pool_m[:, 2 * i:2 * i + 2].reshape(P, 768)
        w = w_pool[2 * i:2 * i + 2].reshape(2, 2, P, PG).transpose(2, 0, 1, 3)
        out[t][:, 768:1792] = w.reshape(P, 1024)
    for kts in ([0, 1, 2, 3, 8, 9, 10, 11], [4, 5, 6, 7, 12, 13, 14, 15]):
        for n in range(4):
            chunk(w_out, n * COLS, kts)
    for part in range(PARTS + 1):
        ups = PART_UP if part < PARTS else LAST_UP
        first = part * PART_KT
        pairs = [np.concatenate([np.arange(f, f + FCH), np.arange(FF + f, FF + f + FCH)])
                 for f in range(first * P, first * P + ups * FCH, FCH)]
        if part == 0:
            in_turn([(w_gate_up, cols) for cols in pairs[:2]])
            pairs = pairs[2:]
        for cols in pairs:
            for g in range(4):
                put(w_gate_up, every[4 * g:4 * g + 4], cols)
        for n in range(4):
            chunk(w_down, n * COLS, list(range(first, first + 2 * ups)))
    assert next(place, None) is None
    return out


def kernel(x, c, w_ada, b_ada, norm_g, w_in, q_gain, k_gain, pe_cmp, w_cmp1, w_cmp2, w_pool, pool_scale,
           w_out, w_gate_up, w_down):
    import concourse.bacc as bacc
    from concourse.bass_utils import run_bass_kernel_spmd

    f = {k: np.ascontiguousarray(v) for k, v in dict(
        x=x, c=c, w_ada=w_ada, b_ada=b_ada, norm_g=norm_g, w_in=w_in, q_gain=q_gain, k_gain=k_gain,
        pe_cmp=pe_cmp, w_cmp1=w_cmp1, w_cmp2=w_cmp2, w_pool=w_pool, pool_scale=pool_scale, w_out=w_out,
        w_gate_up=w_gate_up, w_down=w_down).items()}
    pool_m = pool_matrices()
    stream = np.stack([layer_stream(*[f[n][l] for n in ("w_in", "w_cmp1", "w_cmp2", "w_pool", "w_out",
                                                        "w_gate_up", "w_down")], pool_m)
                       for l in range(DEPTH)])
    SHIFT_SCALE, GATES = (0, 1, 3, 4), (2, 5)
    units = f["w_ada"].reshape(DEPTH, KT, P, 6, 2, 1024).transpose(0, 3, 4, 1, 2, 5)
    order = [(0, v) for v in SHIFT_SCALE[:2]]
    for l in range(DEPTH):
        order.append((l, GATES[0]))
        if l == 0:
            order += [(0, v) for v in SHIFT_SCALE[2:]]
        order.append((l, GATES[1]))
        if l < DEPTH - 1:
            order += [(l + 1, v) for v in SHIFT_SCALE]
    ada = np.stack([units[l, v, i] for l, v in order for i in range(2)])
    b = f["b_ada"].reshape(DEPTH, 6, KT, P)
    gain = f["norm_g"].reshape(DEPTH, 2, KT, P)

    def columns(*vectors):
        return np.concatenate([v.reshape(-1, P) for v in vectors]).T

    vec = np.stack([columns(f["pool_scale"][l], f["q_gain"][l], f["k_gain"][l], f["pe_cmp"][l])
                    for l in range(DEPTH)])
    vec_next = np.stack([columns(*[b[l, v] for v in SHIFT_SCALE], *[gain[l, i // 2] for i in range(4)])
                         for l in range(DEPTH)] + [np.zeros((P, NV_N), np.float32)])
    arrays = {"x": f["x"].reshape(T, D), "stream": stream, "w_ada": ada, "b_ada": f["b_ada"],
              "vec": np.ascontiguousarray(vec), "vec_next": np.ascontiguousarray(vec_next),
              "c_col": np.ascontiguousarray(columns(f["c"])), "const": constants()}
    nc = bacc.Bacc("TRN2", target_bir_lowering=False, num_devices=1)
    args = [nc.dram_tensor(n, a.shape, mybir.dt.from_np(a.dtype), kind="ExternalInput").ap()
            for n, a in arrays.items()]
    out = nc.dram_tensor("out", (T, D), F32, kind="ExternalOutput").ap()
    build(nc, *args, out)
    r = run_bass_kernel_spmd(nc, [arrays], core_ids=[0])
    return r.results[0]["out"].reshape(1, T, D)
```
